# Optimizing a Trainium2 kernel written in Bass

```python
import math
import jax, jax.numpy as jnp
from jax import lax
import numpy as np

D_MODEL = 1024
BATCH = 1
SEQ = 512
DEPTH = 2

CHUNK = 64
Q_BLOCK = 128
NORM_EPS = 1e-5
NEG_INF = -1e30
MAX_POS_OFFSET = 4096

MLA_HEADS = 6
MLA_NOPE = 64
MLA_ROPE = 32
MLA_V = 64
MLA_Q_RANK = 256
MLA_KV_RANK = 128
MLA_WIDTH = MLA_HEADS * MLA_V
ROPE_THETA = 10000.0

SSM_GROUPS = 24
SSM_CH = 16
SSM_STATE = 64
SSM_WIDTH = SSM_GROUPS * SSM_CH
STEP_MIN = 1e-3
STEP_MAX = 1e-1

SB_HEADS = 4
SB_DIM = 64
SB_WIDTH = SB_HEADS * SB_DIM

MIX_WIDTH = MLA_WIDTH + SSM_WIDTH + SB_WIDTH
IN_WIDTHS = (MLA_Q_RANK, MLA_KV_RANK, MLA_ROPE, SSM_WIDTH, SB_WIDTH, SB_WIDTH, SB_WIDTH)
IN_WIDTH = MLA_Q_RANK + MLA_KV_RANK + MLA_ROPE + SSM_WIDTH + 3 * SB_WIDTH

MEM_LEN = 256
MEM_HEADS = 4
MEM_HEAD_DIM = D_MODEL // MEM_HEADS

PEER_HEADS = 8
PEER_N_KEYS = 128
PEER_EXPERTS = PEER_N_KEYS * PEER_N_KEYS
PEER_TOPK = 16
PEER_KEY_DIM = 128
PEER_BLOCK = 128

DN_ALPHA = (2 * DEPTH) ** 0.25
DN_BETA = (8 * DEPTH) ** -0.25

kernel_name = 'hybrid_mla_s5_stickbreak_peer_deepnorm'

def layer_norm(x, g, b):
    xf = x.astype(jnp.float32)
    mu = jnp.mean(xf, axis=-1, keepdims=True)
    var = jnp.mean(jnp.square(xf - mu), axis=-1, keepdims=True)
    return ((xf - mu) * lax.rsqrt(var + NORM_EPS) * g + b).astype(x.dtype)

def group_rms(y):
    yf = y.astype(jnp.float32)
    return (yf * lax.rsqrt(jnp.mean(yf * yf, axis=-1, keepdims=True) + NORM_EPS)).astype(y.dtype)

def rms_norm(x, g):
    return group_rms(x) * g

def split_columns(t, widths):
    outs, start = [], 0
    for w in widths:
        outs.append(t[..., start:start + w])
        start += w
    return outs

def rope(x, pos):
    half = x.shape[-1] // 2
    freq = ROPE_THETA ** (-jnp.arange(half, dtype=jnp.float32) / half)
    ang = pos.astype(jnp.float32)[..., None] * freq
    cos = jnp.cos(ang)[:, :, None, :]
    sin = jnp.sin(ang)[:, :, None, :]
    x1 = x[..., :half].astype(jnp.float32)
    x2 = x[..., half:].astype(jnp.float32)
    return jnp.concatenate([x1 * cos - x2 * sin, x1 * sin + x2 * cos], axis=-1).astype(x.dtype)

def sweep_query_blocks(fn, q):
    bsz, seq = q.shape[0], q.shape[1]
    nblk = seq // Q_BLOCK
    qb = jnp.moveaxis(q.reshape(bsz, nblk, Q_BLOCK, q.shape[2], q.shape[3]), 1, 0)
    out = lax.map(lambda a: fn(a[0], a[1] * Q_BLOCK + jnp.arange(Q_BLOCK)), (qb, jnp.arange(nblk)))
    out = jnp.moveaxis(out, 0, 1)
    return out.reshape(bsz, seq, out.shape[3], out.shape[4])

def chunk_causal_softmax_attention(q, k, v):
    seq = k.shape[1]
    key_chunk = jnp.arange(seq) // CHUNK
    scale = q.shape[-1] ** -0.5

    def block(qi, t):
        allowed = key_chunk[None, :] <= (t // CHUNK)[:, None]
        s = jnp.einsum('bqhd,bshd->bhqs', qi, k).astype(jnp.float32) * scale
        p = jax.nn.softmax(jnp.where(allowed, s, NEG_INF), axis=-1)
        return jnp.einsum('bhqs,bshd->bqhd', p.astype(v.dtype), v)

    return sweep_query_blocks(block, q)

def stick_breaking_attention(q, k, v):
    seq = k.shape[1]
    key_pos = jnp.arange(seq)
    scale = q.shape[-1] ** -0.5

    def block(qi, t):
        earlier = key_pos[None, :] < t[:, None]
        z = jnp.einsum('bqhd,bshd->bhqs', qi, k).astype(jnp.float32) * scale
        log_fail = jnp.where(earlier, jax.nn.log_sigmoid(-z), 0.0)
        log_between = lax.cumsum(log_fail, axis=3, reverse=True) - log_fail
        w = jnp.where(earlier, jnp.exp(jax.nn.log_sigmoid(z) + log_between), 0.0)
        return jnp.einsum('bhqs,bshd->bqhd', w.astype(v.dtype), v)

    return sweep_query_blocks(block, q)

def complex_linear_combine(e1, e2):
    a1r, a1i, b1r, b1i = e1
    a2r, a2i, b2r, b2i = e2
    return (a2r * a1r - a2i * a1i,
            a2r * a1i + a2i * a1r,
            a2r * b1r - a2i * b1i + b2r,
            a2r * b1i + a2i * b1r + b2i)

def s5_glu(u, lam_re, lam_im, log_step, b_re, b_im, c_re, c_im, d_skip, w_glu, b_glu):
    f32 = jnp.float32
    bsz, seq, _ = u.shape
    ug = u.reshape(bsz, seq, SSM_GROUPS, SSM_CH).astype(f32)
    lr, li = lam_re.astype(f32), lam_im.astype(f32)
    step = jnp.exp(log_step.astype(f32))[:, None]
    decay = jnp.exp(lr * step)
    ab_re, ab_im = decay * jnp.cos(li * step), decay * jnp.sin(li * step)
    inv = 1.0 / (lr * lr + li * li)
    f_re = ((ab_re - 1.0) * lr + ab_im * li) * inv
    f_im = (ab_im * lr - (ab_re - 1.0) * li) * inv
    br, bi = b_re.astype(f32), b_im.astype(f32)
    bb_re = f_re[..., None] * br - f_im[..., None] * bi
    bb_im = f_re[..., None] * bi + f_im[..., None] * br
    bu_re = jnp.einsum('bsgh,gph->bsgp', ug, bb_re)
    bu_im = jnp.einsum('bsgh,gph->bsgp', ug, bb_im)
    a_re = jnp.broadcast_to(ab_re, (1, seq) + ab_re.shape)
    a_im = jnp.broadcast_to(ab_im, (1, seq) + ab_im.shape)
    _, _, h_re, h_im = lax.associative_scan(complex_linear_combine, (a_re, a_im, bu_re, bu_im), axis=1)
    y = (jnp.einsum('bsgp,ghp->bsgh', h_re, c_re.astype(f32))
         - jnp.einsum('bsgp,ghp->bsgh', h_im, c_im.astype(f32))
         + d_skip.astype(f32) * ug)
    y = jax.nn.gelu(y.reshape(bsz, seq, SSM_WIDTH))
    y = y * jax.nn.sigmoid(y @ w_glu.astype(f32) + b_glu.astype(f32))
    return y.astype(u.dtype)

def hybrid_mixer(x, positions, w_in, g_cq, g_ckv, w_uq, w_ukv,
                 lam_re, lam_im, log_step, b_re, b_im, c_re, c_im, d_skip,
                 w_glu, b_glu, g_mix, w_out):
    bsz, seq, _ = x.shape
    c_q, c_kv, k_r, u_ssm, q_sb, k_sb, v_sb = split_columns(x @ w_in, IN_WIDTHS)
    q = (rms_norm(c_q, g_cq) @ w_uq).reshape(bsz, seq, MLA_HEADS, MLA_NOPE + MLA_ROPE)
    kv = (rms_norm(c_kv, g_ckv) @ w_ukv).reshape(bsz, seq, MLA_HEADS, MLA_NOPE + MLA_V)
    q = jnp.concatenate([q[..., :MLA_NOPE], rope(q[..., MLA_NOPE:], positions)], axis=-1)
    k_rope = jnp.broadcast_to(rope(k_r[:, :, None, :], positions), (bsz, seq, MLA_HEADS, MLA_ROPE))
    k = jnp.concatenate([kv[..., :MLA_NOPE], k_rope], axis=-1)
    y_mla = chunk_causal_softmax_attention(q, k, kv[..., MLA_NOPE:]).reshape(bsz, seq, MLA_WIDTH)
    y_ssm = s5_glu(u_ssm, lam_re, lam_im, log_step, b_re, b_im, c_re, c_im, d_skip, w_glu, b_glu)
    y_sb = stick_breaking_attention(q_sb.reshape(bsz, seq, SB_HEADS, SB_DIM),
                                    k_sb.reshape(bsz, seq, SB_HEADS, SB_DIM),
                                    v_sb.reshape(bsz, seq, SB_HEADS, SB_DIM)).reshape(bsz, seq, SB_WIDTH)
    y = jnp.concatenate([group_rms(y_mla), group_rms(y_ssm), group_rms(y_sb)], axis=-1) * g_mix
    return y @ w_out

def memory_cross_attention(x, mem, w_mq, w_mkv, w_mo):
    bsz, seq, _ = x.shape
    q = (x @ w_mq).reshape(bsz, seq, MEM_HEADS, MEM_HEAD_DIM)
    k, v = jnp.split((mem @ w_mkv).reshape(mem.shape[0], mem.shape[1], 2, MEM_HEADS, MEM_HEAD_DIM), 2, axis=2)
    k, v = k[:, :, 0], v[:, :, 0]
    s = jnp.einsum('bqhd,bmhd->bhqm', q, k).astype(jnp.float32) * MEM_HEAD_DIM ** -0.5
    p = jax.nn.softmax(s, axis=-1).astype(v.dtype)
    o = jnp.einsum('bhqm,bmhd->bqhd', p, v).reshape(bsz, seq, D_MODEL)
    return o @ w_mo

def peer_ffn(x, w_pq, sub_keys, expert_u, expert_v):
    bsz, seq, d = x.shape
    q = (x @ w_pq).reshape(bsz, seq, PEER_HEADS, 2, PEER_KEY_DIM)
    scores = jnp.einsum('bshcd,hcnd->bshcn', q, sub_keys).astype(jnp.float32)
    top_v, top_i = lax.top_k(scores, PEER_TOPK)
    cand = (top_v[..., 0, :, None] + top_v[..., 1, None, :]).reshape(bsz, seq, PEER_HEADS, PEER_TOPK * PEER_TOPK)
    cand_idx = (top_i[..., 0, :, None] * PEER_N_KEYS + top_i[..., 1, None, :]).reshape(
        bsz, seq, PEER_HEADS, PEER_TOPK * PEER_TOPK)
    best_v, best_pos = lax.top_k(cand, PEER_TOPK)
    idx = jnp.take_along_axis(cand_idx, best_pos, axis=-1)
    gate = jax.nn.softmax(best_v, axis=-1)
    n_tok = bsz * seq
    nblk = n_tok // PEER_BLOCK
    n_sel = PEER_HEADS * PEER_TOPK
    xb = x.reshape(nblk, PEER_BLOCK, d)
    ib = idx.reshape(nblk, PEER_BLOCK, n_sel)
    gb = gate.reshape(nblk, PEER_BLOCK, n_sel).astype(x.dtype)

    def block(args):
        xt, it, gt = args
        h = jax.nn.gelu(jnp.einsum('ted,td->te', expert_u[it], xt))
        return jnp.einsum('te,ted->td', gt * h, expert_v[it])

    return lax.map(block, (xb, ib, gb)).reshape(bsz, seq, d)

def setup_inputs(seed: int = 0) -> dict:
    key = jax.random.key(seed)
    ks = iter(jax.random.split(key, 48))
    f32 = jnp.float32
    L = DEPTH

    def nrm(shape, scale):
        return jax.random.normal(next(ks), shape, f32) * scale

    x = nrm((BATCH, SEQ, D_MODEL), 1.0)
    mem = nrm((BATCH, MEM_LEN, D_MODEL), 1.0)
    offset = jax.random.randint(next(ks), (BATCH, 1), 0, MAX_POS_OFFSET, dtype=jnp.int32)
    positions = offset + jnp.arange(SEQ, dtype=jnp.int32)[None, :]
    n_idx = jnp.arange(SSM_STATE, dtype=f32)
    return {
        'x': x,
        'mem': mem,
        'positions': positions,
        'w_in': nrm((L, D_MODEL, IN_WIDTH), D_MODEL ** -0.5),
        'g_cq': 1.0 + nrm((L, MLA_Q_RANK), 0.02),
        'g_ckv': 1.0 + nrm((L, MLA_KV_RANK), 0.02),
        'w_uq': nrm((L, MLA_Q_RANK, MLA_HEADS * (MLA_NOPE + MLA_ROPE)), MLA_Q_RANK ** -0.5),
        'w_ukv': nrm((L, MLA_KV_RANK, MLA_HEADS * (MLA_NOPE + MLA_V)), MLA_KV_RANK ** -0.5),
        'ssm_lam_re': -0.5 + nrm((L, SSM_GROUPS, SSM_STATE), 0.01),
        'ssm_lam_im': math.pi * n_idx + nrm((L, SSM_GROUPS, SSM_STATE), 0.01),
        'ssm_log_step': jax.random.uniform(next(ks), (L, SSM_GROUPS), f32, math.log(STEP_MIN), math.log(STEP_MAX)),
        'ssm_b_re': nrm((L, SSM_GROUPS, SSM_STATE, SSM_CH), (2 * SSM_CH) ** -0.5),
        'ssm_b_im': nrm((L, SSM_GROUPS, SSM_STATE, SSM_CH), (2 * SSM_CH) ** -0.5),
        'ssm_c_re': nrm((L, SSM_GROUPS, SSM_CH, SSM_STATE), SSM_STATE ** -0.5),
        'ssm_c_im': nrm((L, SSM_GROUPS, SSM_CH, SSM_STATE), SSM_STATE ** -0.5),
        'ssm_d': nrm((L, SSM_GROUPS, SSM_CH), 1.0),
        'w_glu': nrm((L, SSM_WIDTH, SSM_WIDTH), SSM_WIDTH ** -0.5),
        'b_glu': nrm((L, SSM_WIDTH), 0.01),
        'g_mix': 1.0 + nrm((L, MIX_WIDTH), 0.02),
        'w_out': nrm((L, MIX_WIDTH, D_MODEL), MIX_WIDTH ** -0.5 * DN_BETA),
        'ln_mix_g': 1.0 + nrm((L, D_MODEL), 0.02),
        'ln_mix_b': nrm((L, D_MODEL), 0.01),
        'w_mq': nrm((L, D_MODEL, D_MODEL), D_MODEL ** -0.5),
        'w_mkv': nrm((L, D_MODEL, 2 * D_MODEL), D_MODEL ** -0.5),
        'w_mo': nrm((L, D_MODEL, D_MODEL), D_MODEL ** -0.5 * DN_BETA),
        'ln_mem_g': 1.0 + nrm((L, D_MODEL), 0.02),
        'ln_mem_b': nrm((L, D_MODEL), 0.01),
        'w_pq': nrm((L, D_MODEL, PEER_HEADS * 2 * PEER_KEY_DIM), D_MODEL ** -0.5),
        'peer_sub_keys': nrm((L, PEER_HEADS, 2, PEER_N_KEYS, PEER_KEY_DIM), PEER_KEY_DIM ** -0.5),
        'peer_u': nrm((L, PEER_EXPERTS, D_MODEL), D_MODEL ** -0.5),
        'peer_v': nrm((L, PEER_EXPERTS, D_MODEL), PEER_HEADS ** -0.5 * DN_BETA),
        'ln_ffn_g': 1.0 + nrm((L, D_MODEL), 0.02),
        'ln_ffn_b': nrm((L, D_MODEL), 0.01),
    }

def reference(x, mem, positions, w_in, g_cq, g_ckv, w_uq, w_ukv,
              ssm_lam_re, ssm_lam_im, ssm_log_step, ssm_b_re, ssm_b_im, ssm_c_re, ssm_c_im, ssm_d,
              w_glu, b_glu, g_mix, w_out, ln_mix_g, ln_mix_b,
              w_mq, w_mkv, w_mo, ln_mem_g, ln_mem_b,
              w_pq, peer_sub_keys, peer_u, peer_v, ln_ffn_g, ln_ffn_b):
    for l in range(DEPTH):
        mix = hybrid_mixer(x, positions, w_in[l], g_cq[l], g_ckv[l], w_uq[l], w_ukv[l],
                           ssm_lam_re[l], ssm_lam_im[l], ssm_log_step[l], ssm_b_re[l], ssm_b_im[l],
                           ssm_c_re[l], ssm_c_im[l], ssm_d[l], w_glu[l], b_glu[l], g_mix[l], w_out[l])
        x = layer_norm(DN_ALPHA * x + mix, ln_mix_g[l], ln_mix_b[l])
        x = layer_norm(DN_ALPHA * x + memory_cross_attention(x, mem, w_mq[l], w_mkv[l], w_mo[l]),
                       ln_mem_g[l], ln_mem_b[l])
        x = layer_norm(DN_ALPHA * x + peer_ffn(x, w_pq[l], peer_sub_keys[l], peer_u[l], peer_v[l]),
                       ln_ffn_g[l], ln_ffn_b[l])
    return x


_drawn_inputs = setup_inputs


def setup_inputs(seed=0):
    import zlib

    import numpy as np

    out = dict(_drawn_inputs(seed))
    spreads = {}
    factors = {'g_cq': 6.711,
     'g_ckv': 4.604,
     'ssm_lam_re': 8.0,
     'b_glu': 8.0,
     'g_mix': 4.161,
     'ln_mix_b': 2.671,
     'ln_mem_b': 2.7,
     'ln_ffn_b': 2.769}
    for name, (base, spread) in spreads.items():
        noise = np.random.default_rng([zlib.crc32(name.encode()), seed]).standard_normal(out[name].shape)
        drawn = base * np.exp(spread * noise) if base else spread * noise
        out[name] = __import__('jax').numpy.asarray(drawn.astype(out[name].dtype))
    for name, factor in factors.items():
        out[name] = (out[name] * factor).astype(out[name].dtype)
    return out
```

```python
import math
from contextlib import ExitStack

import numpy as np
from concourse import bass, mybir

F32 = mybir.dt.float32
F16 = mybir.dt.float16
I32 = mybir.dt.int32
U32 = mybir.dt.uint32
ACT = mybir.ActivationFunctionType
ALU = mybir.AluOpType
AX = mybir.AxisListType

P = 128
D, SEQ, DEPTH = 1024, 512, 2
KT, NT = D // P, SEQ // P
QR, KVR = 256, 128
MH, NOPE, ROPE, MV = 6, 64, 32, 64
SG, SC, SS = 24, 16, 64
ST = SG * SS // P
BH, BD = 4, 64
MEM, XH, XD = 256, 4, 256
MT = MEM // P
PH, PK, TOP = 8, 128, 16
EB = PK
EPS = 1e-5
ALPHA = (2 * DEPTH) ** 0.25
MLA_SCALE = (NOPE + ROPE) ** -0.5
SB_SCALE = BD ** -0.5
MEM_SCALE = XD ** -0.5
CHUNK = 64
NEG = -1e30
LOWEST = -3e38

WS, XS = 256.0, 16.0
UNSCALE = 1.0 / (WS * XS)
GS = 4096.0

T_CQ, T_CKV, T_KR, T_KRS, T_U, T_QSB, T_KSB, T_VSB, T_OUT = 0, 2, 3, 4, 5, 8, 10, 12, 14
N_IN, N_OUT, N_MK, N_MV, N_MQ, N_MO, N_PQ = 14, 8, 8, 8, 8, 8, 16
T_MK = N_IN + N_OUT
T_PQ = T_MK + N_MK + N_MV + N_MQ + N_MO
N_PROJ = T_PQ + N_PQ
RING = 4


class Named:
    pass


class Steps:

    def __init__(self, eng, sem):
        self.eng, self.sem, self.n = eng, sem, 0

    def __call__(self, ins):
        self.n += 1
        ins.then_inc(self.sem, 1)
        self.eng.wait_ge(self.sem, self.n)

    def restart(self):
        self.eng.sem_clear(self.sem)
        self.n = 0



def load_tile(m, sp, src, r, k):
    sp.wait_ge(m.split_done, r * RING + k + 1)
    sp.dma_start(m.wf[:, k, :], src).then_inc(m.loaded[k], 16)


def split_high(m, act, r, k, slot=None):
    slot = k if slot is None else slot
    act.wait_ge(m.loaded[k], r * 16 + 16)
    act.wait_ge(m.tile_used, r * RING + k + 1)
    m.nc.scalar.activation(m.wh[:, slot, :], m.wf[:, k, :], ACT.Copy, scale=WS).then_inc(m.high_done, 1)


def split_low(m, dve, r, k, slot=None):
    slot = k if slot is None else slot
    dve.wait_ge(m.high_done, r * RING + k + 1)
    m.nc.vector.scalar_tensor_tensor(m.wl[:, slot, :], m.wf[:, k, :], WS, m.wh[:, slot, :],
                                     ALU.mult, ALU.subtract).then_inc(m.split_done, 1)


def start_stream(m, act_slots, eng, who):
    if who == "dve":
        eng.sem_inc(m.split_done, RING)
    if who == "pe":
        eng.sem_inc(m.tile_used, act_slots)


def wait_tile(m, pe, r, k):
    pe.wait_ge(m.split_done, r * RING + k + 1 + RING)


def project(m, out, slot, xh, xl, n):
    wh, wl = (w[:, slot, :].rearrange("p (k c) -> p k c", k=KT) for w in (m.wh, m.wl))
    for k in range(KT):
        m.nc.tensor.matmul(out, wh[:, k, :], xh[:, k, 0:n], start=(k == 0), stop=False)
        m.nc.tensor.matmul(out, wh[:, k, :], xl[:, k, 0:n], start=False, stop=False)
        last = m.nc.tensor.matmul(out, wl[:, k, :], xh[:, k, 0:n], start=False, stop=(k == KT - 1))
    return last


def project_rows(m, outs, slot, xh, xl):
    wh, wl = (w[:, slot, :].rearrange("p (k c) -> p k c", k=KT) for w in (m.wh, m.wl))
    for b, out in enumerate(outs):
        t = slice(b * P, (b + 1) * P)
        for k in range(KT):
            m.nc.tensor.matmul(out, xh[:, k, t], wh[:, k, :], start=(k == 0), stop=False)
            m.nc.tensor.matmul(out, xh[:, k, t], wl[:, k, :], start=False, stop=False)
            last = m.nc.tensor.matmul(out, xl[:, k, t], wh[:, k, :], start=False, stop=(k == KT - 1))
    return last



LN_CHUNKS = 4
LN_W = KT // LN_CHUNKS


def ln_pe(m, pe, bank_sum, bank_var):
    for f in range(KT):
        pe.wait_ge(m.res_added, f + 1)
        last = m.nc.tensor.matmul(bank_sum, m.ones[:, :], m.xT[:, f, :], start=(f == 0), stop=(f == KT - 1))
    last.then_inc(m.ln_sum, 1)
    for c in range(LN_CHUNKS):
        pe.wait_ge(m.ln_sq, c + 1)
        for f in range(LN_W):
            i = c * LN_W + f
            last = m.nc.tensor.matmul(bank_var, m.ones[:, :], m.sq[:, c % 2, f, :], start=(i == 0),
                                      stop=(i == KT - 1))
        last.then_inc(m.ln_var, 1)


def ln_act(m, act, bank_var):
    for c in range(LN_CHUNKS):
        act.wait_ge(m.ln_centred, c + 1)
        if c >= 2:
            act.wait_ge(m.ln_var, c - 1)
        m.nc.scalar.activation(m.sq[:, c % 2, :, :], m.xT[:, c * LN_W:(c + 1) * LN_W, :], ACT.Square)\
            .then_inc(m.ln_sq, 1)
    act.wait_ge(m.ln_var, LN_CHUNKS)
    m.nc.scalar.activation(m.rs[:, 0, :], bank_var, ACT.Sqrt, scale=1.0 / D, bias=m.eps_ln[:, :])\
        .then_inc(m.ln_sd, 1)
    for f in range(KT):
        act.wait_ge(m.ln_out, f + 1)
        m.nc.scalar.activation(m.xh[:, f, :], m.xT[:, f, :], ACT.Copy, scale=XS).then_inc(m.xh_done, 1)


def ln_dve(m, dve, step, bank_sum, g, b):
    dve.wait_ge(m.ln_sum, 1)
    for c in range(LN_CHUNKS):
        x = m.xT[:, c * LN_W:(c + 1) * LN_W, :]
        mean = bank_sum.unsqueeze(1).to_broadcast([P, LN_W, SEQ])
        m.nc.vector.scalar_tensor_tensor(x, mean, -1.0 / D, x, ALU.mult, ALU.add).then_inc(m.ln_centred, 1)
    dve.wait_ge(m.ln_sd, 1)
    step(m.nc.vector.reciprocal(m.rs[:, 1, :], m.rs[:, 0, :]))
    dve.wait_ge(m.ln_centred, LN_CHUNKS)
    dve.wait_ge(m.ln_sq, LN_CHUNKS)
    for c in range(LN_CHUNKS):
        x = m.xT[:, c * LN_W:(c + 1) * LN_W, :]
        step(m.nc.vector.tensor_tensor(x, x, m.rs[:, 1:2, :].to_broadcast([P, LN_W, SEQ]), ALU.mult))
        for f in range(c * LN_W, (c + 1) * LN_W):
            m.nc.vector.tensor_scalar(m.xT[:, f, :], m.xT[:, f, :], g[:, f:f + 1], b[:, f:f + 1],
                                      ALU.mult, ALU.add).then_inc(m.ln_out, 1)
    for f in range(KT):
        dve.wait_ge(m.xh_done, f + 1)
        step(m.nc.vector.scalar_tensor_tensor(m.xl[:, f, :], m.xT[:, f, :], XS, m.xh[:, f, :],
                                              ALU.mult, ALU.subtract))


TWO_PI = 2 * math.pi
PI_1 = 6.28125
PI_2 = float(np.float32(int((TWO_PI - PI_1) * 2 ** 21) / 2 ** 21))
PI_3 = TWO_PI - PI_1 - PI_2
ROUND = 1.5 * 2 ** 23
PI_IN = 3.1415925


def reduce_angle(nc, step, out, turns, ang, quarter):
    step(nc.vector.tensor_scalar(turns, ang, 1 / TWO_PI, 0.25 if quarter else 0.0, ALU.mult, ALU.add))
    step(nc.vector.tensor_scalar(turns, turns, ROUND, None, ALU.add))
    step(nc.vector.tensor_scalar(turns, turns, -ROUND, None, ALU.add))
    step(nc.vector.scalar_tensor_tensor(out, turns, -PI_1, ang, ALU.mult, ALU.add))
    step(nc.vector.scalar_tensor_tensor(out, turns, -PI_2, out, ALU.mult, ALU.add))
    step(nc.vector.scalar_tensor_tensor(out, turns, -PI_3, out, ALU.mult, ALU.add))
    if quarter:
        step(nc.vector.tensor_scalar(out, out, math.pi / 2, None, ALU.add))
    step(nc.vector.tensor_scalar(out, out, PI_IN, -PI_IN, ALU.min, ALU.max))


class Region:

    def __init__(self, tensor, words):
        self.tensor, self.words, self.at = tensor, words, 0

    def take(self, shape, dtype=F32):
        n = int(np.prod(shape)) // (2 if dtype == F16 else 1)
        assert self.at + n <= self.words, (self.at, n, self.words)
        v = self.tensor[:, self.at:self.at + n]
        self.at += n
        if dtype != F32:
            v = v.bitcast(dtype)
        if len(shape) > 1:
            names = "abcd"[:len(shape)]
            v = v.rearrange("p (%s) -> p %s" % (" ".join(names), " ".join(names)),
                            **dict(zip(names, shape)))
        return v


PAR = {}
N_PAR = 0
for _name, _cols in (("g_cq", 2), ("g_ckv", 1), ("g_mix", KT), ("ln_mix_g", KT), ("ln_mix_b", KT),
                     ("ln_mem_g", KT), ("ln_mem_b", KT), ("ln_ffn_g", KT), ("ln_ffn_b", KT),
                     ("b_glu", 3), ("ssm_d", 3), ("lam_re", ST), ("lam_im", ST), ("log_step", ST)):
    PAR[_name] = slice(N_PAR, N_PAR + _cols)
    N_PAR += _cols


def setup(nc, m, a):
    w = Region(m.work, m.words)
    pos = w.take([SEQ], I32)
    posf, ang, turns, arg = (w.take([SEQ]) for _ in range(4))
    with nc.Block() as block:
        @block.sync
        def _(sp):
            sp.dma_start(m.xT[:, :, :], a.x.rearrange("(k p) t -> p k t", p=P)).then_inc(m.s_x, 16)
            sp.dma_start(m.freq[:, :], a.freq).then_inc(m.s_small, 16)
            sp.dma_start(pos[:, :], a.positions.partition_broadcast(P)).then_inc(m.s_small, 16)

        @block.gpsimd
        def _(pool):
            nc.gpsimd.memset(m.ones[:, :], 1.0)
            nc.gpsimd.memset(m.full[:, :], -1.0 / SB_SCALE)
            nc.gpsimd.memset(m.eps[:, :], EPS)
            nc.gpsimd.memset(m.eps_ln[:, :], EPS / ALPHA ** 2).then_inc(m.s_pool, 1)
            nc.gpsimd.iota(m.iota16[:, :], pattern=[[1, TOP]], base=0, channel_multiplier=0,
                           allow_small_or_imprecise_dtypes=True)
            nc.gpsimd.iota(m.iota_rep[:, :, :], pattern=[[1, P], [0, TC]], base=0, channel_multiplier=0,
                           allow_small_or_imprecise_dtypes=True).then_inc(m.s_pool, 1)
            pool.wait_ge(m.s_pool, 2)
            for out, src, op, base, step_, cm, fill in (
                    (m.ident, m.ones, ALU.is_equal, 0, -1, 1, 0.0),
                    (m.tri, m.full, ALU.is_ge, 0, -1, 1, 0.0),
                    (m.before, m.ones, ALU.is_gt, 0, 1, -1, 0.0)):
                nc.gpsimd.affine_select(out=out[:, :], in_=src[:, :], pattern=[[step_, P]], compare_op=op,
                                        fill=fill, base=base, channel_multiplier=cm)

        @block.vector
        def _(dve):
            step = Steps(dve, m.dve_step)
            dve.wait_ge(m.s_small, 32)
            step(nc.vector.tensor_copy(posf[:, :], pos[:, :]))
            step(nc.vector.tensor_scalar(ang[:, :], posf[:, :], m.freq[:, 0:1], None, ALU.mult))
            reduce_angle(nc, step, arg[:, :], turns[:, :], ang[:, :], False)
            step(nc.vector.tensor_copy(m.rs[:, 0, :], arg[:, :]))
            reduce_angle(nc, step, arg[:, :], turns[:, :], ang[:, :], True)
            nc.vector.tensor_copy(m.rs[:, 1, :], arg[:, :]).then_inc(m.s_ang, 1)
            dve.wait_ge(m.s_sin, 1)
            nc.vector.tensor_scalar(m.sinT[:, :], m.sinT[:, :], m.freq[:, 1:2], None, ALU.mult)
            for f in range(KT):
                dve.wait_ge(m.xh_done, f + 1)
                nc.vector.scalar_tensor_tensor(m.xl[:, f, :], m.xT[:, f, :], XS, m.xh[:, f, :],
                                               ALU.mult, ALU.subtract)

        @block.scalar
        def _(act):
            act.wait_ge(m.s_x, 16)
            for f in range(KT):
                nc.scalar.activation(m.xh[:, f, :], m.xT[:, f, :], ACT.Copy, scale=XS).then_inc(m.xh_done, 1)
            act.wait_ge(m.s_ang, 1)
            nc.scalar.activation(m.sinT[:, :], m.rs[:, 0, :], ACT.Sin).then_inc(m.s_sin, 1)
            nc.scalar.activation(m.cosT[:, :], m.rs[:, 1, :], ACT.Sin)


def end_stage(nc, m):
    nc.sync.sem_clear(range(m.sem_first, m.sem_last + 1))
    nc.all_engine_barrier()


def ssm_parameters(m, dve, step, par, v, c, cc):
    nc = m.nc
    lr, li, ls = (par[:, PAR[n]] for n in ("lam_re", "lam_im", "log_step"))
    TT, OP = nc.vector.tensor_tensor, ALU
    dve.wait_ge(m.ssm_exp, 1)
    step(TT(v.th, li, v.step, OP.mult))
    step(TT(v.lrs, lr, v.step, OP.mult))
    reduce_angle(nc, step, v.a0, v.t0, v.th, False)
    reduce_angle(nc, step, v.a1, v.t0, v.th, True)
    dve.sem_inc(m.ssm_args, 1)
    dve.wait_ge(m.ssm_trig, 1)
    step(TT(v.re, v.r, v.cos, OP.mult))
    step(TT(v.im, v.r, v.sin, OP.mult))
    step(nc.vector.tensor_scalar(v.re, v.re, -1.0, None, OP.add))
    step(TT(v.t0, lr, lr, OP.mult))
    step(TT(v.t1, li, li, OP.mult))
    step(TT(v.t0, v.t0, v.t1, OP.add))
    step(nc.vector.reciprocal(v.inv, v.t0))
    step(TT(v.t0, v.re, lr, OP.mult))
    step(TT(v.t1, v.im, li, OP.mult))
    step(TT(v.t0, v.t0, v.t1, OP.add))
    step(TT(v.fre, v.t0, v.inv, OP.mult))
    step(TT(v.t0, v.im, lr, OP.mult))
    step(TT(v.t1, v.re, li, OP.mult))
    step(TT(v.t0, v.t0, v.t1, OP.subtract))
    step(TT(v.fim, v.t0, v.inv, OP.mult))
    dve.wait_ge(m.weights, 16 * N_SMALL)
    wide = [P, ST, 2 * SC]
    fre, fim = (x.unsqueeze(2).to_broadcast(wide) for x in (v.fre, v.fim))
    t = v.wide
    step(TT(t[:, 0], c[:, 0], fre, OP.mult))
    step(TT(t[:, 1], c[:, 1], fim, OP.mult))
    step(TT(cc[:, 0], t[:, 0], t[:, 1], OP.subtract))
    step(TT(cc[:, 1], t[:, 1], t[:, 0], OP.subtract))
    step(TT(t[:, 0], c[:, 0], fim, OP.mult))
    step(TT(t[:, 1], c[:, 1], fre, OP.mult))
    step(nc.vector.scalar_tensor_tensor(cc[:, 2], t[:, 0], -1.0, t[:, 1], OP.mult, OP.subtract))


N_SMALL = 6
PAIRS = ST // 2


def sb_cols(a):
    return {0: 0, 1: 512, 3: 896, 2: 1024}[a], SEQ - P * a


SB_W = 1280


def mixer(nc, m, a, layer):
    w = Region(m.work, m.words)
    par = w.take([N_PAR])
    lat = w.take([3, SEQ])
    cq, ckv = lat[:, 0:2, :], lat[:, 2:3, :]
    glu = lat.rearrange("p a t -> p (a t)")[:, 0:9 * P].rearrange("p (a c) -> p a c", a=3)
    kr, u = w.take([2, SEQ]), w.take([3, SEQ])
    qsb, ksb, vsb = w.take([2, SEQ]), w.take([2, SEQ]), w.take([NT, BH * BD])
    qh, kh, vm = w.take([MH, SEQ]), w.take([MH, SEQ]), w.take([NT, MH * MV])
    uq, ukv = w.take([2, 768]), w.take([768])
    bz = w.take([2, 3, 2, P])
    cc = w.take([3, ST, 2 * SC])
    tab = [x.rearrange("p k t -> p (k t)").bitcast(F32).rearrange("p (z a t) -> p z a t", z=2, a=2)
           for x in (m.xh[:, :, :], m.xl[:, :, :])]
    both = w.take([4, SEQ])
    vv, gg = both[:, 0:2, :], both[:, 2:4, :]
    grs = both[:, 0:3, :]
    share = w.at
    sp_, rl, wt = w.take([SB_W]), w.take([SB_W]), w.take([SB_W])
    w.at = share
    prob, probT = w.take([2, SEQ]), w.take([2, SEQ])
    w.at = share
    rt, cz = w.take([4, SEQ]), w.take([2, ST, 2 * SC])
    pr = m.sq
    small = Region(m.small, 2624)
    tmp = small.take([2, 2, SEQ // 2])
    v = Named()
    (v.step, v.th, v.lrs, v.a0, v.a1, v.t0, v.t1, v.sin, v.cos, v.r, v.re, v.im, v.inv, v.fre,
     v.fim) = (small.take([ST]) for _ in range(15))
    v.wide = small.take([2, ST, 2 * SC])
    mx, nmx, rsum, rinv = (small.take([2]) for _ in range(4))
    y = [qh[:, 2 * j, :] for j in range(3)] + [u[:, j, :] for j in range(3)] + [qsb[:, j, :] for j in range(2)]
    B = [m.ps[:, b, :] for b in range(8)]
    TT, STT, TS = nc.vector.tensor_tensor, nc.vector.scalar_tensor_tensor, nc.vector.tensor_scalar
    MM = nc.tensor.matmul
    EVAC = N_IN + 10
    dest = [cq[:, 0, :], cq[:, 1, :], ckv[:, 0, :], kr[:, 0, :], kr[:, 1, :], u[:, 0, :], u[:, 1, :],
            u[:, 2, :], qsb[:, 0, :], qsb[:, 1, :], ksb[:, 0, :], ksb[:, 1, :]]
    iters = [(h, b) for h in range(MH) for b in range(NT)]

    with nc.Block() as block:
        @block.sync
        def _(sp):
            sp.dma_start(par[:, :], a.par[layer]).then_inc(m.params, 16)
            for n in range(N_IN + N_OUT):
                load_tile(m, sp, a.proj[layer, n], n // RING, n % RING)
                if n == 3:
                    for dst, src in ((uq, a.uq), (ukv, a.ukv), (bz, a.bz), (cz, a.cz)):
                        flat = dst if len(dst.shape) == 2 else dst.rearrange(
                            {3: "p a b -> p (a b)", 4: "p a b c -> p (a b c)",
                             5: "p a b c d -> p (a b c d)"}[len(dst.shape)])
                        sp.dma_start(flat, src[layer]).then_inc(m.weights, 16)
                    for z, dst in enumerate((qh, kh)):
                        sp.dma_start(dst[96:P, :, :], a.mask[:, z:z + 1, :].to_broadcast([32, MH, SEQ]))\
                            .then_inc(m.weights, 16)

        @block.tensor
        def _(pe):
            start_stream(m, RING, pe, "pe")
            for n in range(N_IN):
                wait_tile(m, pe, n // RING, n % RING)
                if n >= 2:
                    pe.wait_ge(m.evac, n - 1)
                if n < T_VSB:
                    last = project(m, B[n % 2], n % RING, m.xh, m.xl, SEQ)
                else:
                    last = project_rows(m, [B[n % 2][:, b * P:(b + 1) * P] for b in range(NT)], n % RING,
                                        m.xh, m.xl)
                last.then_inc(m.tile_used, 1)
                if n == T_KRS + 1:
                    pe.wait_ge(m.lat_sq, 2)
                    for c in range(2):
                        MM(B[2], m.ones[:, :], rt[:, c, :], start=(c == 0), stop=(c == 1))
                    pe.wait_ge(m.lat_sq, 3)
                    MM(B[3], m.ones[:, :], rt[:, 2, :], start=True, stop=True).then_inc(m.lat_sum, 1)
            pe.wait_ge(m.weights, 16 * N_SMALL)
            pe.wait_ge(m.lat_done, 3)
            for i in range(3):
                pe.wait_ge(m.evac, N_IN + i - 1)
                for c in range(2):
                    last = MM(B[(N_IN + i) % 2], uq[:, c, i * P:(i + 1) * P], cq[:, c, :],
                              start=(c == 0), stop=(c == 1))
                last.then_inc(m.up, 1)
            for i in range(3):
                pe.wait_ge(m.evac, N_IN + 3 + i - 1)
                MM(B[(N_IN + 3 + i) % 2], ukv[:, i * P:(i + 1) * P], ckv[:, 0, :], start=True, stop=True)\
                    .then_inc(m.up, 1)
            for b in range(NT):
                pe.wait_ge(m.evac, N_IN + 6 + b - 1)
                MM(B[(N_IN + 6 + b) % 2][:, 0:MH * MV], ckv[:, 0, b * P:(b + 1) * P], ukv[:, MH * NOPE:],
                   start=True, stop=True).then_inc(m.up, 1)
            for r in range(2):
                for s in range(2):
                    o = MH * NOPE + (2 * s + r) * 96
                    for c in range(2):
                        last = MM(B[4 + 2 * r + s][0:96, :], uq[:, c, o:o + 96], cq[:, c, :],
                                  start=(c == 0), stop=(c == 1))
                last.then_inc(m.rot, 1)
            pe.wait_ge(m.rot_done, 1)
            pe.wait_ge(m.evac, EVAC)

            def ssm_in(st):
                j, q = st // 4, st % 4
                if st >= 1:
                    pe.wait_ge(m.ssm_mul, st)
                rows = slice(64 * (q // 2), 64 * (q // 2) + 64)
                for z in range(2):
                    last = MM(B[z], bz[rows, z, j, q % 2, :], u[rows, j, :], start=True, stop=True)
                last.then_inc(m.ssm_bu, 1)

            def ssm_out(st):
                j, q = st // 4, st % 4
                pe.wait_ge(m.ssm_prod, st + 1)
                if q == 0 and j >= 1:
                    pe.wait_ge(m.ssm_y, j)
                out = B[2][32 * q:32 * q + 32, :]
                for i, (z, lhs) in enumerate((((0, 0), 0), ((1, 1), 1), ((1, 0), 2), ((0, 1), 2))):
                    last = MM(out, cc[:, lhs, st, :], pr[:, z[0], z[1], :], start=(i == 0), stop=(i == 3))
                last.then_inc(m.ssm_read, 1)

            def sb_scores(h, stop):
                rows = slice(64 * (h % 2), 64 * (h % 2) + 64)
                for s in range(NT):
                    o, n = sb_cols(s)
                    last = MM(m.zb[:, o:o + n], ksb[rows, h // 2, s * P:(s + 1) * P],
                              qsb[rows, h // 2, s * P:], start=True, stop=True)
                return last

            for h in range(BH):
                ssm_in(h)
                if h >= 1:
                    pe.wait_ge(m.sb_w, h)
                sb_scores(h, True).then_inc(m.sb_z, 1)
                if h >= 1:
                    ssm_out(h - 1)
                pe.wait_ge(m.sb_sp, h + 1)
                rows = slice(64 * (h % 2), 64 * (h % 2) + 64)
                for s in range(NT):
                    o, n = sb_cols(s)
                    MM(m.zb[:, o:o + n], ksb[rows, h // 2, s * P:(s + 1) * P], qsb[rows, h // 2, s * P:],
                       start=True, stop=False)
                    last = MM(m.zb[:, o:o + n], m.tri[:, :], sp_[:, o:o + n], start=False, stop=(s == NT - 1))
                    for s2 in range(s + 1, NT):
                        o2, n2 = sb_cols(s2)
                        last = MM(m.zb[:, o + n - n2:o + n], m.full[:, :], sp_[:, o2:o2 + n2],
                                  start=False, stop=(s2 == NT - 1))
                last.then_inc(m.sb_t, 1)
                pe.wait_ge(m.sb_wm, h + 1)
                if h == 2:
                    pe.wait_ge(m.sb_y, 1)
                for s in range(NT):
                    o, n = sb_cols(s)
                    last = MM(B[7][rows, s * P:], vsb[:, s, h * BD:(h + 1) * BD], wt[:, o:o + n],
                              start=(s == 0), stop=(s == NT - 1))
                last.then_inc(m.sb_o, 1)
            ssm_out(BH - 1)

            def mla_s(i):
                h, b = iters[i]
                if i >= 2:
                    pe.wait_ge(m.mla_e, i - 1)
                n = P * (b + 1)
                MM(B[4 + i % 2][:, 0:n], qh[:, h, b * P:n], kh[:, h, 0:n], start=True, stop=True)\
                    .then_inc(m.mla_sc, 1)

            def mla_t(i):
                h, b = iters[i]
                pe.wait_ge(m.mla_p, i + 1)
                if i >= 2:
                    pe.wait_ge(m.mla_pt, i - 1)
                for c in range(b + 1):
                    last = nc.tensor.transpose(B[(3, 6)[i % 2]][:, c * P:(c + 1) * P],
                                               prob[:, i % 2, c * P:(c + 1) * P], m.ident[:, :])
                last.then_inc(m.mla_tr, 1)

            def mla_o(i):
                h, b = iters[i]
                pe.wait_ge(m.mla_pt, i + 1)
                if h % 2 == 0 and b == 0:
                    if h == 0:
                        pe.wait_ge(m.sb_y, 2)
                    else:
                        pe.wait_ge(m.mla_y, h // 2)
                rows = slice(64 * (h % 2), 64 * (h % 2) + 64)
                for c in range(b + 1):
                    last = MM(B[7][rows, b * P:(b + 1) * P], vm[:, c, h * MV:(h + 1) * MV],
                              probT[:, i % 2, c * P:(c + 1) * P], start=(c == 0), stop=(c == b))
                last.then_inc(m.mla_av, 1)

            for i in range(len(iters)):
                mla_s(i)
                if i % 3 == 0:
                    ssm_in(BH + i // 3)
                if i >= 1:
                    mla_t(i - 1)
                if i >= 2:
                    mla_o(i - 2)
                if i % 3 == 0 and i >= 3:
                    ssm_out(BH + i // 3 - 1)
            mla_t(len(iters) - 1)
            mla_o(len(iters) - 2)
            mla_o(len(iters) - 1)
            ssm_out(ST - 1)
            pe.wait_ge(m.glu_in, 16)
            pe.wait_ge(m.gelu_done, 3)
            for j in range(3):
                for c in range(3):
                    last = MM(B[j], glu[:, c, j * P:(j + 1) * P], u[:, c, :], start=(c == 0), stop=(c == 2))
                last.then_inc(m.glu_mm, 1)
            for i, (g, c, n) in enumerate([(1, c, 2) for c in range(2)] + [(0, c, 3) for c in range(3)]
                                          + [(2, c, 3) for c in range(3)]):
                pe.wait_ge(m.grp_sq, i + 1)
                last = MM(B[4 + g], m.ones[:, :], m.sqf[:, i % 4, :], start=(c == 0), stop=(c == n - 1))
                last.then_inc(m.grp_sum, 1)
            for f in range(N_OUT):
                n = N_IN + f
                if f == 0:
                    pe.wait_ge(m.yl_done, KT)
                wait_tile(m, pe, n // RING, n % RING)
                if f >= 2:
                    pe.wait_ge(m.res_added, f - 1)
                project(m, B[f % 2], n % RING, m.xh, m.xl, SEQ).then_inc(m.tile_used, 1)
            ln_pe(m, pe, B[2], B[3])

        @block.scalar
        def _(act):
            AF = nc.scalar.activation
            act.wait_ge(m.params, 16)
            AF(v.step, par[:, PAR["log_step"]], ACT.Exp).then_inc(m.ssm_exp, 1)
            for n in range(RING):
                split_high(m, act, 0, n)
            for n in range(N_IN):
                act.wait_ge(m.tile_used, n + 1 + RING)
                if n < T_VSB:
                    AF(dest[n], B[n % 2], ACT.Copy, scale=UNSCALE).then_inc(m.evac, 1)
                else:
                    c = (n - T_VSB) * P
                    AF(vsb[:, :, c:c + P], B[n % 2].rearrange("p (b c) -> p b c", b=NT), ACT.Copy,
                       scale=UNSCALE).then_inc(m.evac, 1)
                if n < N_IN + N_OUT - RING:
                    split_high(m, act, (n + RING) // RING, n % RING)
                if n <= 2:
                    act.wait_ge(m.evac, n + 1)
                    AF(rt[:, n, :], dest[n], ACT.Square).then_inc(m.lat_sq, 1)
                if n == T_KRS + 2:
                    act.wait_ge(m.lat_sum, 1)
                    AF(m.rs[:, 0, :], B[2], ACT.Sqrt, scale=1.0 / QR, bias=m.eps[:, :])
                    AF(m.rs[:, 1, :], B[3], ACT.Sqrt, scale=1.0 / KVR, bias=m.eps[:, :]).then_inc(m.lat_sd, 1)
            act.wait_ge(m.ssm_args, 1)
            AF(v.sin, v.a0, ACT.Sin)
            AF(v.cos, v.a1, ACT.Sin)
            AF(v.r, v.lrs, ACT.Exp).then_inc(m.ssm_trig, 1)
            for i in range(10):
                act.wait_ge(m.up, i + 1)
                bank = B[(N_IN + i) % 2]
                if i < 6:
                    for z in range(2):
                        last = AF((qh, kh)[i // 3][0:NOPE, 2 * (i % 3) + z, :], bank[64 * z:64 * z + 64, :], ACT.Copy)
                else:
                    last = AF(vm[:, i - 6, :], bank[:, 0:MH * MV], ACT.Copy)
                last.then_inc(m.evac, 1)
            act.wait_ge(m.rot_done, 1)
            act.dma_start(glu, a.glu[layer].rearrange("p (a c) -> p a c", a=3)).then_inc(m.glu_in, 16)
            for h in range(BH):
                act.wait_ge(m.sb_z, h + 1)
                if h >= 1:
                    act.wait_ge(m.sb_t, h)
                AF(sp_[:, :], m.zb[:, 0:SB_W], ACT.Abs, scale=SB_SCALE).then_inc(m.act_step, 1)
                act.wait_ge(m.act_step, 3 * h + 1)
                AF(sp_[:, :], sp_[:, :], ACT.Exp, scale=-1.0).then_inc(m.act_step, 1)
                act.wait_ge(m.act_step, 3 * h + 2)
                AF(sp_[:, :], sp_[:, :], ACT.Ln, bias=1.0).then_inc(m.act_step, 1)
                act.wait_ge(m.sb_t, h + 1)
                if h >= 1:
                    act.wait_ge(m.sb_o, h)
                AF(wt[:, :], m.zb[:, 0:SB_W], ACT.Exp, scale=SB_SCALE).then_inc(m.sb_w, 1)
                if h % 2 == 1:
                    act.wait_ge(m.sb_o, h + 1)
                    AF(y[6 + h // 2], B[7], ACT.Copy).then_inc(m.sb_y, 1)
            for i, (h, b) in enumerate(iters):
                n = P * (b + 1)
                act.wait_ge(m.mla_nm, i + 1)
                if i >= 2:
                    act.wait_ge(m.mla_tr, i - 1)
                if i == 0:
                    act.wait_ge(m.sb_o, BH)
                AF(prob[:, i % 2, 0:n], B[4 + i % 2][:, 0:n], ACT.Exp, scale=MLA_SCALE,
                   bias=nmx[:, i % 2:i % 2 + 1], accum_out=rsum[:, i % 2:i % 2 + 1]).then_inc(m.mla_e, 1)
                if i >= 1:
                    mla_copy(m, act, i - 1, iters, probT, B)
                if i >= 3 and iters[i - 3][1] == NT - 1 and iters[i - 3][0] % 2 == 1:
                    mla_out(m, act, i - 3, iters, y, B)
            mla_copy(m, act, len(iters) - 1, iters, probT, B)
            mla_out(m, act, len(iters) - 1, iters, y, B)
            for j in range(3):
                act.wait_ge(m.ssm_y, j + 1)
                AF(u[:, j, :], u[:, j, :], ACT.Gelu_apprx_tanh).then_inc(m.gelu_done, 1)
            for j in range(3):
                act.wait_ge(m.glu_mm, j + 1)
                AF(m.sqf[:, j, :], B[j], ACT.Sigmoid, bias=par[:, PAR["b_glu"]][:, j:j + 1]).then_inc(m.glu_sig, 1)
            order = [6, 7, 0, 1, 2, 3, 4, 5]
            for i, f in enumerate(order):
                if i == 0:
                    act.wait_ge(m.sb_y, 2)
                    act.wait_ge(m.mla_y, 3)
                    act.wait_ge(m.glu_done, 3)
                if i >= 4:
                    act.wait_ge(m.grp_sum, i - 3)
                AF(m.sqf[:, i % 4, :], y[f], ACT.Square).then_inc(m.grp_sq, 1)
            for k, (g, need, width) in enumerate(((1, 2, BH * BD), (0, 5, MH * MV), (2, 8, SG * SC))):
                act.wait_ge(m.grp_sum, need)
                AF(grs[:, k, :], B[4 + g], ACT.Sqrt, scale=1.0 / width,
                   bias=m.eps[:, :]).then_inc(m.grp_sd, 1)
            for f in range(KT):
                act.wait_ge(m.y_norm, f + 1)
                if f == 0:
                    act.wait_ge(m.tile_used, N_IN + RING)
                AF(m.xh[:, f, :], y[f], ACT.Copy, scale=XS).then_inc(m.yh_done, 1)
            for f in range(N_OUT - RING):
                n = N_IN + RING + f
                split_high(m, act, n // RING, n % RING)
            ln_act(m, act, B[3])

        @block.gpsimd
        def _(pool):
            PT = nc.gpsimd.tensor_tensor
            step = Steps(pool, m.pool_step)
            pool.wait_ge(m.ssm_trig, 1)
            pool.wait_ge(m.tile_used, N_IN + RING)
            for q in range(PAIRS):
                c, s = tab[q % 2][:, 0], tab[q % 2][:, 1]
                if q >= 2:
                    pool.wait_ge(m.ssm_prod, 2 * (q - 1))
                nc.gpsimd.memset(c[:, :, 0:1], 1.0)
                nc.gpsimd.memset(s[:, :, 0:1], 0.0)
                nc.gpsimd.tensor_copy(c[:, :, 1:2], v.cos[:, 2 * q:2 * q + 2].unsqueeze(2))
                step(nc.gpsimd.tensor_copy(s[:, :, 1:2], v.sin[:, 2 * q:2 * q + 2].unsqueeze(2)))
                n = 1
                while n < SEQ:
                    k = min(n, SEQ - 1 - n)
                    lo, hi = slice(1, 1 + k), slice(n + 1, n + 1 + k)
                    cn, sn = (x[:, :, n:n + 1].to_broadcast([P, 2, k]) for x in (c, s))
                    t0, t1 = (tmp[:, z, :, 0:k] for z in range(2))
                    PT(t0, c[:, :, lo], cn, ALU.mult)
                    step(PT(t1, s[:, :, lo], sn, ALU.mult))
                    step(PT(c[:, :, hi], t0, t1, ALU.subtract))
                    PT(t0, s[:, :, lo], cn, ALU.mult)
                    step(PT(t1, c[:, :, lo], sn, ALU.mult))
                    step(PT(s[:, :, hi], t0, t1, ALU.add))
                    n *= 2
                pool.sem_inc(m.table, 1)

        @block.vector
        def _(dve):
            step = Steps(dve, m.dve_step)
            start_stream(m, RING, dve, "dve")
            for n in range(RING):
                split_low(m, dve, 0, n)
            for n in range(N_IN):
                split_low(m, dve, (n + RING) // RING, n % RING)
            dve.wait_ge(m.lat_sd, 1)
            step(nc.vector.reciprocal(m.rs[:, :, :], m.rs[:, :, :]))
            for c in range(2):
                STT(cq[:, c, :], cq[:, c, :], par[:, PAR["g_cq"]][:, c:c + 1], m.rs[:, 0, :], ALU.mult,
                    ALU.mult).then_inc(m.lat_done, 1)
            STT(ckv[:, 0, :], ckv[:, 0, :], par[:, PAR["g_ckv"]], m.rs[:, 1, :], ALU.mult, ALU.mult)\
                .then_inc(m.lat_done, 1)
            ssm_parameters(m, dve, step, par, v, cz, cc)
            dve.wait_ge(m.evac, T_KRS + 1)
            TT(rt[:, 0, :], kr[:, 0, :], m.cosT[:, :], ALU.mult)
            step(TT(rt[:, 1, :], kr[:, 1, :], m.sinT[:, :], ALU.mult))
            step(TT(kh[64:96, :, :], rt[64:96, 0:1, :].to_broadcast([32, MH, SEQ]),
                    rt[64:96, 1:2, :].to_broadcast([32, MH, SEQ]), ALU.add))
            for r in range(2):
                dve.wait_ge(m.rot, r + 1)
                TT(rt[0:96, 2, :], B[4 + 2 * r][0:96, :], m.cosT[0:96, :], ALU.mult)
                step(TT(rt[0:96, 3, :], B[5 + 2 * r][0:96, :], m.sinT[0:96, :], ALU.mult))
                for z in range(3):
                    last = TT(qh[64:96, 3 * r + z, :], rt[32 * z:32 * z + 32, 2, :],
                              rt[32 * z:32 * z + 32, 3, :], ALU.add)
                step(last)
            dve.sem_inc(m.rot_done, 1)

            def ssm_forward(st):
                c, s = (tab[(st // 2) % 2][:, z, st % 2, :].unsqueeze(1).to_broadcast([P, 2, SEQ])
                        for z in range(2))
                dve.wait_ge(m.table, st // 2 + 1)
                dve.wait_ge(m.ssm_bu, st + 1)
                if st >= 1:
                    dve.wait_ge(m.ssm_read, st)
                TT(pr[:, 0], m.ps[:, 0:2, :], c, ALU.mult)
                TT(pr[:, 1], m.ps[:, 0:2, :], s, ALU.mult).then_inc(m.ssm_mul, 1)
                dve.wait_ge(m.ssm_mul, st + 1)
                TT(vv[:, 0, :], pr[:, 0, 0, :], pr[:, 1, 1, :], ALU.add)
                step(TT(vv[:, 1, :], pr[:, 0, 1, :], pr[:, 1, 0, :], ALU.subtract))

            def ssm_scan(st):
                decay = v.r[:, st:st + 1].to_broadcast([P, SEQ])
                for z in range(2):
                    last = nc.vector.tensor_tensor_scan(gg[:, z, :], decay, vv[:, z, :], 0.0, ALU.mult, ALU.add)
                step(last)

            def ssm_back(st):
                c, s = (tab[(st // 2) % 2][:, z, st % 2, :].unsqueeze(1).to_broadcast([P, 2, SEQ])
                        for z in range(2))
                TT(pr[:, 0], gg[:, :, :], c, ALU.mult)
                TT(pr[:, 1], gg[:, :, :], s, ALU.mult).then_inc(m.ssm_prod, 1)

            def ssm_skip(st):
                if st > 0 and st % 4 == 3:
                    j = st // 4
                    dve.wait_ge(m.ssm_read, st + 1)
                    STT(u[:, j, :], u[:, j, :], par[:, PAR["ssm_d"]][:, j:j + 1], B[2], ALU.mult, ALU.add)\
                        .then_inc(m.ssm_y, 1)

            for h in range(BH):
                ssm_forward(h)
                dve.wait_ge(m.act_step, 3 * h + 1)
                step(TS(rl[:, :], m.zb[:, 0:SB_W], SB_SCALE, 0.0, ALU.mult, ALU.max))
                ssm_scan(h)
                dve.wait_ge(m.act_step, 3 * (h + 1))
                step(TT(sp_[:, :], sp_[:, :], rl[:, :], ALU.add))
                for s in range(NT):
                    o, _n = sb_cols(s)
                    last = TT(sp_[:, o:o + P], sp_[:, o:o + P], m.before[:, :], ALU.mult)
                last.then_inc(m.sb_sp, 1)
                ssm_back(h)
                ssm_skip(h - 1)
                dve.wait_ge(m.sb_w, h + 1)
                for s in range(NT):
                    o, _n = sb_cols(s)
                    last = TT(wt[:, o:o + P], wt[:, o:o + P], m.before[:, :], ALU.mult)
                last.then_inc(m.sb_wm, 1)
            ssm_skip(BH - 1)
            for i, (h, b) in enumerate(iters):
                n, k = P * (b + 1), i % 2
                dve.wait_ge(m.mla_sc, i + 1)
                step(nc.vector.reduce_max(mx[:, k:k + 1], B[4 + k][:, 0:n], AX.X))
                if i >= 2:
                    dve.wait_ge(m.mla_e, i - 1)
                TS(nmx[:, k:k + 1], mx[:, k:k + 1], -MLA_SCALE, None, ALU.mult).then_inc(m.mla_nm, 1)
                st = BH + i // 3
                if i % 3 == 0:
                    if i >= 3:
                        ssm_skip(st - 1)
                    ssm_forward(st)
                elif i % 3 == 1:
                    ssm_scan(st)
                else:
                    ssm_back(st)
                dve.wait_ge(m.mla_e, i + 1)
                step(nc.vector.reciprocal(rinv[:, k:k + 1], rsum[:, k:k + 1]))
                TS(prob[:, k, 0:n], prob[:, k, 0:n], rinv[:, k:k + 1], None, ALU.mult).then_inc(m.mla_p, 1)
            ssm_skip(ST - 1)
            for j in range(3):
                dve.wait_ge(m.glu_sig, j + 1)
                dve.wait_ge(m.glu_mm, 3)
                TT(u[:, j, :], u[:, j, :], m.sqf[:, j, :], ALU.mult).then_inc(m.glu_done, 1)
            dve.wait_ge(m.grp_sd, 3)
            dve.wait_ge(m.grp_sq, 8)
            step(nc.vector.reciprocal(grs[:, :, :], grs[:, :, :]))
            for f in range(KT):
                k = 1 if f < 3 else 2 if f < 6 else 0
                STT(y[f], y[f], par[:, PAR["g_mix"]][:, f:f + 1], grs[:, k, :], ALU.mult, ALU.mult)\
                    .then_inc(m.y_norm, 1)
            for f in range(KT):
                dve.wait_ge(m.yh_done, f + 1)
                STT(m.xl[:, f, :], y[f], XS, m.xh[:, f, :], ALU.mult, ALU.subtract).then_inc(m.yl_done, 1)
            for f in range(N_OUT):
                if f < N_OUT - RING:
                    n = N_IN + RING + f
                    split_low(m, dve, n // RING, n % RING)
                dve.wait_ge(m.tile_used, N_IN + f + 1 + RING)
                STT(m.xT[:, f, :], B[f % 2], UNSCALE / ALPHA, m.xT[:, f, :], ALU.mult, ALU.add)\
                    .then_inc(m.res_added, 1)
            ln_dve(m, dve, step, B[2], par[:, PAR["ln_mix_g"]], par[:, PAR["ln_mix_b"]])
    end_stage(nc, m)


def mla_copy(m, act, i, iters, probT, B):
    n = P * (iters[i][1] + 1)
    act.wait_ge(m.mla_tr, i + 1)
    if i >= 2:
        act.wait_ge(m.mla_av, i - 1)
    m.nc.scalar.activation(probT[:, i % 2, 0:n], B[(3, 6)[i % 2]][:, 0:n], ACT.Copy).then_inc(m.mla_pt, 1)


def mla_out(m, act, i, iters, y, B):
    act.wait_ge(m.mla_av, i + 1)
    m.nc.scalar.activation(y[iters[i][0] // 2], B[7], ACT.Copy).then_inc(m.mla_y, 1)


def memory(nc, m, a, layer):
    w = Region(m.work, m.words)
    par = w.take([N_PAR])
    memf = w.take([KT, MEM])
    mh, ml = w.take([KT, MEM], F16), w.take([KT, MEM], F16)
    km, vm, q = w.take([KT, MEM]), w.take([MT, D]), w.take([KT, SEQ])
    prob, probT = w.take([2, MEM]), w.take([2, MT, SEQ])
    small = Region(m.small, 1400)
    mx, nmx, rsum, rinv = (small.take([2]) for _ in range(4))
    B = [m.ps[:, b, :] for b in range(8)]
    STT, TS = nc.vector.scalar_tensor_tensor, nc.vector.tensor_scalar
    MM = nc.tensor.matmul
    iters = [(h, b) for h in range(XH) for b in range(NT)]
    R_MV, R_MQ, R_MO = N_MK // RING, (N_MK + N_MV) // RING, (N_MK + N_MV + N_MQ) // RING
    R_END = R_MO + N_MO // RING
    PAIR = XD // P

    with nc.Block() as block:
        @block.sync
        def _(sp):
            sp.dma_start(par[:, :], a.par[layer]).then_inc(m.params, 16)
            sp.dma_start(memf[:, :, :], a.mem.rearrange("(k p) t -> p k t", p=P)).then_inc(m.weights, 16)
            with sp.Fori(0, R_END) as r:
                for k in range(RING):
                    load_tile(m, sp, a.proj[layer, r * RING + (T_MK + k)], r, k)

        @block.tensor
        def _(pe):
            start_stream(m, RING, pe, "pe")
            pe.wait_ge(m.weights, 17)

            def segment(r0, emit):
                with pe.Fori(r0, r0 + 2) as r:
                    for k in range(RING):
                        wait_tile(m, pe, r, k)
                        pe.wait_ge(m.evac, r * RING + k + 1)
                        emit(k).then_inc(m.tile_used, 1)

            segment(0, lambda k: project(m, B[k % 2][:, 0:MEM], k, mh, ml, MEM))
            segment(R_MV, lambda k: project_rows(m, [B[k % 2][:, b * P:(b + 1) * P] for b in range(MT)],
                                                 k, mh, ml))
            segment(R_MQ, lambda k: project(m, B[k % 2], k, m.xh, m.xl, SEQ))
            pe.wait_ge(m.evac, R_MO * RING + 2)

            def scores(i):
                h, b = iters[i]
                if i >= 2:
                    pe.wait_ge(m.mla_e, i - 1)
                for c in range(PAIR):
                    last = MM(B[2 + i % 2][:, 0:MEM], q[:, PAIR * h + c, b * P:(b + 1) * P],
                              km[:, PAIR * h + c, :], start=(c == 0), stop=(c == PAIR - 1))
                last.then_inc(m.mla_sc, 1)

            def turn(i):
                pe.wait_ge(m.mla_p, i + 1)
                if i >= 2:
                    pe.wait_ge(m.mla_pt, i - 1)
                for c in range(MT):
                    last = nc.tensor.transpose(B[4 + i % 2][:, c * P:(c + 1) * P],
                                               prob[:, i % 2, c * P:(c + 1) * P], m.ident[:, :])
                last.then_inc(m.mla_tr, 1)

            def values(h):
                pe.wait_ge(m.mla_pt, NT * (h + 1))
                for f in range(PAIR):
                    n = PAIR * h + f
                    if n >= 2:
                        pe.wait_ge(m.yl_done, n - 1)
                    for c in range(MT):
                        last = MM(B[6 + f], vm[:, c, n * P:(n + 1) * P], probT[:, h % 2, c, :],
                                  start=(c == 0), stop=(c == MT - 1))
                    last.then_inc(m.mla_av, 1)

            for i, (h, b) in enumerate(iters):
                scores(i)
                if i >= 1:
                    turn(i - 1)
                if b == 1 and h >= 1:
                    values(h - 1)
            turn(len(iters) - 1)
            values(XH - 1)
            for f in range(N_MO):
                if f == 0:
                    pe.wait_ge(m.yl_done, KT)
                wait_tile(m, pe, R_MO + f // RING, f % RING)
                if f >= 2:
                    pe.wait_ge(m.res_added, f - 1)
                project(m, B[f % 2], f % RING, m.xh, m.xl, SEQ).then_inc(m.tile_used, 1)
            ln_pe(m, pe, B[2], B[3])

        @block.scalar
        def _(act):
            AF = nc.scalar.activation
            act.sem_inc(m.evac, 2)
            act.wait_ge(m.weights, 16)
            AF(mh[:, :, :], memf[:, :, :], ACT.Copy, scale=XS).then_inc(m.xh_mem, 1)
            for k in range(RING):
                split_high(m, act, 0, k)

            def segment(r0, dst):
                with act.Fori(0, 2) as s:
                    for k in range(RING):
                        act.wait_ge(m.tile_used, s * RING + (r0 * RING + k + 1 + RING))
                        dst(s, k).then_inc(m.evac, 1)
                        split_high(m, act, s + (r0 + 1), k)

            segment(0, lambda s, k: AF(km[:, bass.ds(s * RING + k, 1), :],
                                       m.ps[:, k % 2:k % 2 + 1, 0:MEM], ACT.Copy, scale=UNSCALE))
            segment(R_MV, lambda s, k: AF(vm[:, :, bass.ds((s * RING + k) * P, P)],
                                          B[k % 2][:, 0:MEM].rearrange("p (b c) -> p b c", b=MT),
                                          ACT.Copy, scale=UNSCALE))
            segment(R_MQ, lambda s, k: AF(q[:, bass.ds(s * RING + k, 1), :],
                                          m.ps[:, k % 2:k % 2 + 1, :], ACT.Copy, scale=UNSCALE))

            def exps(i):
                act.wait_ge(m.mla_nm, i + 1)
                if i >= 2:
                    act.wait_ge(m.mla_tr, i - 1)
                AF(prob[:, i % 2, :], B[2 + i % 2][:, 0:MEM], ACT.Exp, scale=MEM_SCALE,
                   bias=nmx[:, i % 2:i % 2 + 1], accum_out=rsum[:, i % 2:i % 2 + 1]).then_inc(m.mla_e, 1)

            def copy(i):
                h, b = iters[i]
                act.wait_ge(m.mla_tr, i + 1)
                if h >= 2 and b == 0:
                    act.wait_ge(m.mla_av, PAIR * (h - 1))
                AF(probT[:, h % 2, :, b * P:(b + 1) * P],
                   B[4 + i % 2][:, 0:MEM].rearrange("p (c t) -> p c t", c=MT), ACT.Copy)\
                    .then_inc(m.mla_pt, 1)

            def high(h):
                for f in range(PAIR):
                    n = PAIR * h + f
                    act.wait_ge(m.mla_av, n + 1)
                    AF(m.xh[:, n, :], B[6 + f], ACT.Copy, scale=XS).then_inc(m.yh_done, 1)

            for i, (h, b) in enumerate(iters):
                exps(i)
                if i >= 1:
                    copy(i - 1)
                if b == 2 and h >= 1:
                    high(h - 1)
            copy(len(iters) - 1)
            high(XH - 1)
            for k in range(RING):
                split_high(m, act, R_END - 1, k)
            ln_act(m, act, B[3])

        @block.vector
        def _(dve):
            step = Steps(dve, m.dve_step)
            start_stream(m, RING, dve, "dve")
            dve.wait_ge(m.xh_mem, 1)
            STT(ml[:, :, :], memf[:, :, :], XS, mh[:, :, :], ALU.mult, ALU.subtract).then_inc(m.weights, 1)
            with dve.Fori(0, R_MO + 1) as r:
                for k in range(RING):
                    split_low(m, dve, r, k)

            def low(h):
                for f in range(PAIR):
                    n = PAIR * h + f
                    dve.wait_ge(m.yh_done, n + 1)
                    STT(m.xl[:, n, :], B[6 + f], XS, m.xh[:, n, :], ALU.mult, ALU.subtract)\
                        .then_inc(m.yl_done, 1)

            for i, (h, b) in enumerate(iters):
                k = i % 2
                dve.wait_ge(m.mla_sc, i + 1)
                step(nc.vector.reduce_max(mx[:, k:k + 1], B[2 + k][:, 0:MEM], AX.X))
                if i >= 2:
                    dve.wait_ge(m.mla_e, i - 1)
                TS(nmx[:, k:k + 1], mx[:, k:k + 1], -MEM_SCALE, None, ALU.mult).then_inc(m.mla_nm, 1)
                dve.wait_ge(m.mla_e, i + 1)
                step(nc.vector.reciprocal(rinv[:, k:k + 1], rsum[:, k:k + 1]))
                TS(prob[:, k, :], prob[:, k, :], rinv[:, k:k + 1], None, ALU.mult).then_inc(m.mla_p, 1)
                if b == 3 and h >= 1:
                    low(h - 1)
            low(XH - 1)
            for f in range(N_MO):
                if f < RING:
                    split_low(m, dve, R_END - 1, f)
                dve.wait_ge(m.tile_used, R_MO * RING + f + 1 + RING)
                STT(m.xT[:, f, :], B[f % 2], UNSCALE / ALPHA, m.xT[:, f, :], ALU.mult, ALU.add)\
                    .then_inc(m.res_added, 1)
            dve.wait_ge(m.params, 16)
            ln_dve(m, dve, step, B[2], par[:, PAR["ln_mem_g"]], par[:, PAR["ln_mem_b"]])
    end_stage(nc, m)


TC = 8
CPT = P // TC
R_PQ = N_PQ // RING
R_TOK = EB // RING // NT
R_SEL = R_TOK // 2


def select(nc, m, a, layer):
    w = Region(m.work, m.words)
    scores = w.take([NT, PH * 2, PK])
    stage = w.take([PK, P])
    keys = stage.rearrange("p a b -> p (a b)")[:, 0:PH * 2 * PK].rearrange("p (h n) -> p h n", h=PH * 2)
    qb, gst = w.take([2, SEQ]), w.take([2, SEQ])
    hot = m.sq.rearrange("p a b t -> p (a b t)").bitcast(F16)
    hot2 = qb.rearrange("p a t -> p (a t)").bitcast(F16)
    hot3 = w.take([2 * P * TC], F16)
    eqb = [hot[:, z * P * TC:(z + 1) * P * TC].rearrange("p (i t) -> p i t", i=P) for z in range(2)]
    ahi = [hot[:, (2 + z) * P * TC:(3 + z) * P * TC].rearrange("p (i t) -> p i t", i=P) for z in range(2)]
    alo = [hot2[:, z * P * TC:(z + 1) * P * TC].rearrange("p (i t) -> p i t", i=P) for z in range(2)]
    bhot = [hot3[:, z * P * TC:(z + 1) * P * TC].rearrange("p (i t) -> p i t", i=P) for z in range(2)]
    eqf = m.sq.rearrange("p a b t -> p (a b t)").rearrange("p (h s c) -> p h s c", h=PH, s=TOP)
    s = Region(m.small, 1400 + 1024)
    sin = s.take([2, PK])
    wk, wk2 = s.take([PK]), s.take([TOP * TOP])
    cand = s.take([TOP, TOP])
    tv, ti, tif = s.take([PH * 2, TOP]), s.take([PH * 2, TOP], U32), s.take([PH * 2, TOP])
    bv, bp = s.take([PH, TOP]), s.take([PH, TOP], U32)
    nb, gsum, ginv = (s.take([PH]) for _ in range(3))
    gate, first, second = (m.rs[:, :, :].rearrange("p a t -> p (a t)")[:, z * P:(z + 1) * P] for z in range(3))
    ib = m.rs[:, :, :].rearrange("p a t -> p (a t)")[:, 3 * P:4 * P].bitcast(U32)
    ibf = m.rs[:, :, :].rearrange("p a t -> p (a t)")[:, 4 * P:5 * P]
    tr = m.rs[:, :, :].rearrange("p a t -> p (a t)")[:, 5 * P:7 * P].bitcast(F16)
    firstT, secondT, ghi, glo = (tr[:, z * P:(z + 1) * P] for z in range(4))
    B = [m.ps[:, b, :] for b in range(8)]
    TT, STT, TS = nc.vector.tensor_tensor, nc.vector.scalar_tensor_tensor, nc.vector.tensor_scalar
    MM = nc.tensor.matmul

    with nc.Block() as block:
        @block.sync
        def _(sp):
            sp.dma_start(keys, a.keys[layer]).then_inc(m.weights, 16)
            with sp.Fori(0, R_PQ) as r:
                for k in range(RING):
                    load_tile(m, sp, a.proj[layer, r * RING + (T_PQ + k)], r, k)
            with sp.Fori(0, EB // RING + 1) as r:
                for k in range(RING):
                    load_tile(m, sp, a.experts[layer, r * RING + k], r + R_PQ, k)

        @block.tensor
        def _(pe):
            start_stream(m, RING, pe, "pe")
            pe.sem_inc(m.scored, 2)
            pe.sem_inc(m.spread, 2)
            pe.wait_ge(m.weights, 16)

            def score(r, k):
                pe.wait_ge(m.evac, r * RING + (k + 1 + 2))
                pe.wait_ge(m.sc_copied, r * RING + (k + 1))
                for b in range(NT):
                    last = MM(B[2 + k % 2][:, b * P:(b + 1) * P], qb[:, k % 2, b * P:(b + 1) * P],
                              keys[:, bass.ds(r * RING + k, 1), :].rearrange("p a n -> p (a n)"),
                              start=True, stop=True)
                last.then_inc(m.scored, 1)

            def projected(r, k):
                wait_tile(m, pe, r, k)
                pe.wait_ge(m.evac, r * RING + (k + 1))
                project(m, B[k % 2], k, m.xh, m.xl, SEQ).then_inc(m.tile_used, 1)

            with pe.Fori(0, R_PQ) as r:
                for k in range(RING):
                    projected(r, k)
                    if k:
                        score(r, k - 1)
                score(r, RING - 1)
            with pe.Fori(0, NT) as tt:
                with pe.Fori(0, R_SEL) as i:
                    for k in range(RING):
                        projected(tt * R_TOK + i + R_PQ, k)
                pe.wait_ge(m.selected, tt + 1)
                for z, x in enumerate((first, second, gate)):
                    last = nc.tensor.transpose(B[2][:, z * P:(z + 1) * P], x, m.ident[:, :])
                last.then_inc(m.sel_turned, 1)
                with pe.Fori(0, CPT // RING) as i:
                    for k in range(RING):
                        projected(tt * R_TOK + i + (R_PQ + R_SEL), k)
                        n = tt * CPT + i * RING + (k + 1)
                        pe.wait_ge(m.hot_first, n)
                        pe.wait_ge(m.hot_second, n)
                        pe.wait_ge(m.staged, n)
                        for t in range(TC):
                            out = B[4 + 2 * (k % 2) + t // 4][:, (t % 4) * P:(t % 4 + 1) * P]
                            MM(out, bhot[k % 2][:, :, t], ahi[k % 2][:, :, t], start=True, stop=False)
                            last = MM(out, bhot[k % 2][:, :, t], alo[k % 2][:, :, t], start=False, stop=True)
                        last.then_inc(m.spread, 1)

        @block.scalar
        def _(act):
            AF = nc.scalar.activation
            act.sem_inc(m.evac, 2)
            act.sem_inc(m.staged, 2)
            for s in (m.g_out[0], m.g_out[1], m.w_out):
                act.sem_inc(s, 1)
            for k in range(RING):
                split_high(m, act, 0, k)
            with act.Fori(0, R_PQ) as r:
                for k in range(RING):
                    act.wait_ge(m.tile_used, r * RING + (k + 1 + RING))
                    act.wait_ge(m.scored, r * RING + (k + 1))
                    AF(qb[:, k % 2, :], B[k % 2], ACT.Copy, scale=UNSCALE).then_inc(m.evac, 1)
                    split_high(m, act, r + 1, k)

            def hidden(r, k):
                act.wait_ge(m.tile_used, r * RING + (k + 1 + RING))
                act.wait_ge(m.g_out[k % 2], (r - R_PQ) * 32 + (16 * (k // 2) + 1))
                AF(gst[:, k % 2, :], B[k % 2], ACT.Gelu_apprx_tanh, scale=UNSCALE).then_inc(m.evac, 1)
                split_high(m, act, r + 1, k)
                act.wait_ge(m.evac, r * RING + (k + 1 + 2))
                act.dma_start(m.hid[r * RING + (k - R_PQ * RING)], gst[:, k % 2, :])\
                    .then_inc(m.g_out[k % 2], 16)

            def gate_exp(tt, h):
                act.wait_ge(m.best, tt * PH + (h + 1))
                AF(gate[:, h * TOP:(h + 1) * TOP], bv[:, h, :], ACT.Exp, bias=nb[:, h:h + 1],
                   accum_out=gsum[:, h:h + 1]).then_inc(m.gate_e, 1)

            act.wait_ge(m.sc_copied, N_PQ + 2)
            with act.Fori(0, NT) as tt:
                for hc in range(2 * PH):
                    hidden(tt * R_TOK + (hc // RING + R_PQ), hc % RING)
                    act.wait_ge(m.sel_used, tt * 2 * PH + (hc + 1))
                    AF(sin[:, hc % 2:hc % 2 + 1, :],
                       scores[:, bass.ds(tt, 1), hc:hc + 1, :].rearrange("p a h n -> p (a h) n"),
                       ACT.Copy).then_inc(m.sel_in, 1)
                    if hc >= 2 and hc % 2 == 0:
                        gate_exp(tt, hc // 2 - 1)
                gate_exp(tt, PH - 1)
                act.wait_ge(m.sel_turned, tt + 1)
                AF(firstT, B[2][:, 0:P], ACT.Copy).then_inc(m.sel_high, 1)
                AF(secondT, B[2][:, P:2 * P], ACT.Copy).then_inc(m.sel_high, 1)
                AF(ghi, B[2][:, 2 * P:3 * P], ACT.Copy, scale=GS).then_inc(m.sel_high, 1)
                act.wait_ge(m.w_out, tt * 16 + 1)
                with act.Fori(0, CPT // RING) as i:
                    for k in range(RING):
                        hidden(tt * R_TOK + i + (R_PQ + R_SEL), k)
                        act.wait_ge(m.spread, tt * CPT + i * RING + (k + 1 + 2))
                        dst = stage.rearrange("p i t -> p t i")[:, bass.ds(i * (RING * TC) + k * TC, TC), :]
                        AF(dst, m.ps[:, 4 + 2 * (k % 2):6 + 2 * (k % 2), :].rearrange(
                            "p z (t i) -> p (z t) i", i=P), ACT.Copy, scale=1 / GS).then_inc(m.staged, 1)
                act.wait_ge(m.staged, tt * CPT + (CPT + 2))
                act.dma_start(m.gates[:, :, bass.ds(tt * P, P)].rearrange("i j t -> j i t"), stage[:, :, :])\
                    .then_inc(m.w_out, 16)
            act.wait_ge(m.w_out, 16 * NT + 1)
            for z in range(2):
                act.wait_ge(m.g_out[z], 16 * EB // 2 + 1)

        @block.gpsimd
        def _(pool):
            step = Steps(pool, m.pool_step)
            with pool.Fori(0, NT) as tt:
                with pool.Fori(0, CPT // 2) as i:
                    step.restart()
                    for k in range(2):
                        pool.wait_ge(m.sel_high, tt * 3 + 2)
                        pool.wait_ge(m.spread, tt * CPT + i * 2 + (k + 1))
                        t = secondT[:, bass.ds(i * (2 * TC) + k * TC, TC)].unsqueeze(1).to_broadcast([P, P, TC])
                        step(nc.gpsimd.tensor_tensor(bhot[k], m.iota_rep[:, :, :], t, ALU.subtract))
                        nc.gpsimd.tensor_scalar(bhot[k], bhot[k], 0.0, None, ALU.is_equal)\
                            .then_inc(m.hot_second, 1)

        @block.vector
        def _(dve):
            V = nc.vector
            step = Steps(dve, m.dve_step)
            start_stream(m, RING, dve, "dve")
            dve.sem_inc(m.sc_copied, 2)
            dve.sem_inc(m.sel_used, 2)
            for k in range(RING):
                split_low(m, dve, 0, k)
            with dve.Fori(0, R_PQ) as r:
                for k in range(RING):
                    split_low(m, dve, r + 1, k)
                    dve.wait_ge(m.scored, r * RING + (k + 1 + 2))
                    V.tensor_copy(scores[:, :, bass.ds(r * RING + k, 1), :].rearrange("p b a n -> p b (a n)"),
                                  B[2 + k % 2].rearrange("p (b n) -> p b n", b=NT)).then_inc(m.sc_copied, 1)

            def top16(vals, idx, src, work):
                step(V.max(vals[:, 0:8], src))
                V.max_index(idx[:, 0:8], vals[:, 0:8], src)
                step(V.match_replace(work, vals[:, 0:8], src, LOWEST))
                step(V.max(vals[:, 8:16], work))
                return V.max_index(idx[:, 8:16], vals[:, 8:16], work)

            wide = [P, PH, TOP, TOP]

            def picked(out, side):
                step(V.tensor_copy(ibf, ib))
                place = ibf.rearrange("p (h s) -> p h s", h=PH).unsqueeze(3).to_broadcast(wide)
                step(TT(eqf, place, m.iota16[:, :].unsqueeze(1).unsqueeze(1).to_broadcast(wide), ALU.is_equal))
                step(TT(eqf, eqf, tif[:, side:PH * 2:2, :].unsqueeze(2).to_broadcast(wide), ALU.mult))
                return V.reduce_sum(out.rearrange("p (h s) -> p h s", h=PH), eqf, AX.X)

            with dve.Fori(0, NT) as tt:
                for hc in range(2 * PH):
                    step.restart()
                    dve.wait_ge(m.sel_in, tt * 2 * PH + (hc + 1))
                    split_low(m, dve, tt * R_TOK + (hc // RING + R_PQ + 1), hc % RING)
                    top16(tv[:, hc, :], ti[:, hc, :], sin[:, hc % 2, :], wk).then_inc(m.sel_used, 1)
                    if hc % 2:
                        h = hc // 2
                        step(TT(cand[:, :, :], tv[:, hc - 1, :].unsqueeze(2).to_broadcast([P, TOP, TOP]),
                                tv[:, hc, :].unsqueeze(1).to_broadcast([P, TOP, TOP]), ALU.add))
                        top16(bv[:, h, :], bp[:, h, :], cand.rearrange("p a b -> p (a b)"), wk2)
                        TS(nb[:, h:h + 1], bv[:, h, 0:1], -1.0, None, ALU.mult).then_inc(m.best, 1)
                dve.wait_ge(m.best, tt * PH + PH)
                dve.wait_ge(m.gate_e, tt * PH + PH)
                step(V.reciprocal(ginv, gsum))
                TT(gate.rearrange("p (h s) -> p h s", h=PH), gate.rearrange("p (h s) -> p h s", h=PH),
                   ginv.unsqueeze(2).to_broadcast([P, PH, TOP]), ALU.mult)
                V.tensor_copy(tif[:, :, :], ti[:, :, :])
                bpf = bp.rearrange("p h s -> p (h s)")
                step(TS(ib, bpf, 4, None, ALU.logical_shift_right))
                dve.wait_ge(m.spread, tt * CPT + 2)
                picked(first, 0)
                step(TS(ib, bpf, TOP - 1, None, ALU.bitwise_and))
                picked(second, 1).then_inc(m.selected, 1)
                dve.wait_ge(m.sel_high, tt * 3 + 3)
                step(STT(glo, B[2][:, 2 * P:3 * P], GS, ghi, ALU.mult, ALU.subtract))
                with dve.Fori(0, CPT // RING) as i:
                    step.restart()
                    for k in range(RING):
                        split_low(m, dve, tt * R_TOK + i + (R_PQ + R_SEL + 1), k)
                        dve.wait_ge(m.spread, tt * CPT + i * RING + (k + 1))
                        t, hi, lo = (x[:, bass.ds(i * (RING * TC) + k * TC, TC)].unsqueeze(1)
                                     .to_broadcast([P, P, TC]) for x in (firstT, ghi, glo))
                        step(TT(eqb[k % 2], m.iota_rep[:, :, :], t, ALU.is_equal))
                        TT(ahi[k % 2], eqb[k % 2], hi, ALU.mult)
                        TT(alo[k % 2], eqb[k % 2], lo, ALU.mult).then_inc(m.hot_first, 1)
    end_stage(nc, m)


GROUP = 4
NG = EB // GROUP


def outputs(nc, m, a, layer):
    w = Region(m.work, m.words)
    par = w.take([N_PAR])
    wh1, wl1 = w.take([RING, D], F16), w.take([RING, D], F16)
    gw = w.take([GROUP, 2, SEQ])
    ph, pl = w.take([2, GROUP, SEQ], F16), w.take([2, GROUP, SEQ], F16)
    wh, wl = (m.wh, wh1), (m.wl, wl1)
    B = [m.ps[:, b, :] for b in range(8)]
    TT, STT = nc.vector.tensor_tensor, nc.vector.scalar_tensor_tensor

    with nc.Block() as block:
        @block.sync
        def _(sp):
            sp.dma_start(par[:, :], a.par[layer]).then_inc(m.params, 16)

            def group(g, first=False):
                for b in range(GROUP):
                    if not first:
                        load_tile(m, sp, a.experts[layer, g * GROUP + (EB + b)], g, b)
                    sp.wait_ge(m.gw_used, g * GROUP + (b + 1))
                    sp.dma_start(gw[:, b, 0, :], m.hid[g * GROUP + b]).then_inc(m.gw_in[b], 16)
                    sp.dma_start(gw[:, b, 1, :], m.gates[g * GROUP + b]).then_inc(m.gw_in[b], 16)

            group(0, True)
            with sp.Fori(1, NG) as g:
                group(g)

        @block.tensor
        def _(pe):
            start_stream(m, 2 * RING, pe, "pe")

            def group(g, z):
                pe.wait_ge(m.split_done, g * GROUP + (GROUP + RING))
                pe.wait_ge(m.prod_done, g * GROUP + GROUP)
                for f in range(KT):
                    pe.wait_ge(m.out_added, g * KT + (f + 1))
                    for b in range(GROUP):
                        c = slice(f * P, (f + 1) * P)
                        nc.tensor.matmul(B[f], wh[z][:, b, c], ph[:, z, b, :], start=(b == 0), stop=False)
                        nc.tensor.matmul(B[f], wh[z][:, b, c], pl[:, z, b, :], start=False, stop=False)
                        last = nc.tensor.matmul(B[f], wl[z][:, b, c], ph[:, z, b, :], start=False,
                                                stop=(b == GROUP - 1))
                    last.then_inc(m.out_done, 1)
                pe.wait_ge(m.out_done, g * KT + KT)
                pe.sem_inc(m.tile_used, GROUP)

            with pe.Fori(0, NG // 2) as i:
                group(i * 2, 0)
                group(i * 2 + 1, 1)
            ln_pe(m, pe, B[0], B[1])

        @block.scalar
        def _(act):
            def group(g, z, first=False):
                for b in range(GROUP):
                    if not first:
                        act.wait_ge(m.loaded[b], g * 16)
                        act.wait_ge(m.tile_used, g * GROUP + (b + 1))
                        nc.scalar.activation(wh[z][:, b, :], m.wf[:, b, :], ACT.Copy, scale=WS)\
                            .then_inc(m.high_done, 1)
                    act.wait_ge(m.multiplied, g * GROUP + (b + 1))
                    act.wait_ge(m.tile_used, g * GROUP + (b + 1))
                    nc.scalar.activation(ph[:, z, b, :], gw[:, b, 0, :], ACT.Copy, scale=XS)\
                        .then_inc(m.prod_high, 1)

            group(0, 0, True)
            with act.Fori(0, NG // 2 - 1) as i:
                group(i * 2 + 1, 1)
                group(i * 2 + 2, 0)
            group(NG - 1, 1)
            ln_act(m, act, B[1])

        @block.vector
        def _(dve):
            step = Steps(dve, m.dve_step)
            dve.sem_inc(m.split_done, 2 * RING)
            dve.sem_inc(m.out_added, KT)
            dve.sem_inc(m.gw_used, GROUP)

            def add(g, f):
                dve.wait_ge(m.out_done, g * KT + (f + 1))
                return STT(m.xT[:, f, :], B[f], UNSCALE / ALPHA, m.xT[:, f, :], ALU.mult, ALU.add)

            def prepare(g, z, before, first=False):
                for b in range(GROUP):
                    dve.wait_ge(m.gw_in[b], g * 32 + 32)
                    TT(gw[:, b, 0, :], gw[:, b, 0, :], gw[:, b, 1, :], ALU.mult).then_inc(m.multiplied, 1)
                    if not first:
                        dve.wait_ge(m.high_done, g * GROUP + (b + 1 - GROUP))
                        STT(wl[z][:, b, :], m.wf[:, b, :], WS, wh[z][:, b, :], ALU.mult, ALU.subtract)\
                            .then_inc(m.split_done, 1)
                        for f in (2 * b, 2 * b + 1):
                            add(before, f).then_inc(m.out_added, 1)
                    dve.wait_ge(m.prod_high, g * GROUP + (b + 1))
                    STT(pl[:, z, b, :], gw[:, b, 0, :], XS, ph[:, z, b, :], ALU.mult, ALU.subtract)\
                        .then_inc(m.prod_done, 1)
                    dve.wait_ge(m.prod_done, g * GROUP + (b + 1))
                    dve.sem_inc(m.gw_used, 1)

            prepare(0, 0, None, True)
            with dve.Fori(0, NG // 2 - 1) as i:
                prepare(i * 2 + 1, 1, i * 2)
                prepare(i * 2 + 2, 0, i * 2 + 1)
            prepare(NG - 1, 1, NG - 2)
            for f in range(KT):
                add(NG - 1, f).then_inc(m.res_added, 1)
            dve.wait_ge(m.params, 16)
            ln_dve(m, dve, step, B[0], par[:, PAR["ln_ffn_g"]], par[:, PAR["ln_ffn_b"]])
    end_stage(nc, m)


INPUTS = "x mem positions freq mask par proj experts keys uq ukv glu bz cz".split()
SEMAPHORES = """split_done tile_used high_done params weights s_x s_small s_pool s_ang s_sin evac lat_sq lat_sum
lat_sd lat_done up rot rot_done ssm_exp ssm_args ssm_trig table ssm_bu ssm_mul ssm_prod ssm_read
ssm_y sb_z sb_sp sb_t sb_w sb_wm sb_o sb_y mla_sc mla_nm mla_e mla_p mla_tr mla_pt mla_av mla_y
gelu_done glu_in glu_mm glu_sig glu_done grp_sq grp_sum grp_sd y_norm yh_done yl_done res_added
ln_sum ln_centred ln_sq ln_var ln_sd ln_out xh_done xh_mem act_step dve_step pool_step scored
sc_copied sel_in sel_used best gate_e selected sel_turned sel_high hot_first hot_second spread
staged w_out gw_used multiplied prod_high prod_done out_added out_done""".split()


def program(nc, inputs, out, depth=DEPTH, stages=4):
    with ExitStack() as ctx:
        def sb(name, shape, dt=F32):
            return ctx.enter_context(nc.sbuf_tensor(name, shape, dt))

        a = Named()
        (a.x, a.mem, a.positions, a.freq, a.mask, a.par, a.proj, a.experts, a.keys, a.uq, a.ukv, a.glu, a.bz,
         a.cz) = (inputs[n] for n in INPUTS)
        m = Named()
        m.nc = nc
        sems = [ctx.enter_context(nc.semaphore(name)) for name in SEMAPHORES]
        (m.split_done, m.tile_used, m.high_done, m.params, m.weights, m.s_x, m.s_small, m.s_pool,
         m.s_ang, m.s_sin, m.evac, m.lat_sq, m.lat_sum, m.lat_sd, m.lat_done, m.up, m.rot, m.rot_done,
         m.ssm_exp, m.ssm_args, m.ssm_trig, m.table, m.ssm_bu, m.ssm_mul, m.ssm_prod, m.ssm_read,
         m.ssm_y, m.sb_z, m.sb_sp, m.sb_t, m.sb_w, m.sb_wm, m.sb_o, m.sb_y, m.mla_sc, m.mla_nm, m.mla_e,
         m.mla_p, m.mla_tr, m.mla_pt, m.mla_av, m.mla_y, m.gelu_done, m.glu_in, m.glu_mm, m.glu_sig,
         m.glu_done, m.grp_sq, m.grp_sum, m.grp_sd, m.y_norm, m.yh_done, m.yl_done, m.res_added,
         m.ln_sum, m.ln_centred, m.ln_sq, m.ln_var, m.ln_sd, m.ln_out, m.xh_done, m.xh_mem, m.act_step,
         m.dve_step, m.pool_step, m.scored, m.sc_copied, m.sel_in, m.sel_used, m.best, m.gate_e,
         m.selected, m.sel_turned, m.sel_high, m.hot_first, m.hot_second, m.spread, m.staged, m.w_out,
         m.gw_used, m.multiplied, m.prod_high, m.prod_done, m.out_added, m.out_done) = sems
        m.loaded = [ctx.enter_context(nc.semaphore(f"loaded{k}")) for k in range(RING)]
        m.g_out = [ctx.enter_context(nc.semaphore(f"g_out{k}")) for k in range(2)]
        m.gw_in = [ctx.enter_context(nc.semaphore(f"gw_in{k}")) for k in range(GROUP)]
        nums = [s.num for s in [*sems, *m.loaded, *m.g_out, *m.gw_in]]
        m.sem_first, m.sem_last = min(nums), max(nums)
        assert m.sem_last - m.sem_first + 1 == len(nums)
        m.s_out = ctx.enter_context(nc.semaphore("s_out"))
        m.xT = sb("xT", [P, KT, SEQ])
        m.xh, m.xl = sb("xh", [P, KT, SEQ], F16), sb("xl", [P, KT, SEQ], F16)
        m.wf = sb("wf", [P, RING, D])
        m.wh, m.wl = sb("wh", [P, RING, D], F16), sb("wl", [P, RING, D], F16)
        m.sq = sb("sq", [P, 2, LN_W, SEQ])[:, :, :, :]
        m.sqf = m.sq.rearrange("p a b t -> p (a b) t")
        m.rs = sb("rs", [P, 2, SEQ])
        m.ident, m.ones, m.full, m.tri, m.before = (
            sb(n, [P, P]) for n in ("ident", "ones", "full", "tri", "before"))
        m.eps, m.eps_ln, m.freq = sb("eps", [P, 1]), sb("eps_ln", [P, 1]), sb("freq_sb", [P, 2])
        m.iota16, m.iota_rep = sb("iota16", [P, TOP]), sb("iota_rep", [P, P, TC], F16)
        m.cosT, m.sinT = sb("cosT", [P, SEQ]), sb("sinT", [P, SEQ])
        m.small = sb("small", [P, 2624])
        m.words = 28100
        m.work = sb("work", [P, m.words])
        m.ps = ctx.enter_context(nc.psum_tensor("ps", [P, 8, SEQ], F32))
        m.zb = m.ps[:, 4:7, :].rearrange("p b t -> p (b t)")
        m.gates = nc.dram_tensor("gates", (EB, P, SEQ), F32, kind="Internal").ap()
        m.hid = nc.dram_tensor("hid", (EB, P, SEQ), F32, kind="Internal").ap()

        setup(nc, m, a)
        end_stage(nc, m)
        with nc.Fori(0, depth) as layer:
            for stage in (mixer, memory, select, outputs)[:stages]:
                stage(nc, m, a, layer)
        with nc.Block() as block:
            @block.sync
            def _(sp):
                sp.dma_start(out.rearrange("(k p) t -> p k t", p=P), m.xT[:, :, :]).then_inc(m.s_out, 16)
                sp.wait_ge(m.s_out, 16)



def column_tiles(w):
    n = w.shape[-1] // P
    return w.reshape(DEPTH, KT, P, n, P).transpose(0, 3, 2, 1, 4).reshape(DEPTH, n, P, KT * P)


def swap_halves(w):
    return np.concatenate([w[..., ROPE // 2:], w[..., :ROPE // 2]], axis=-1)


def layouts(i):
    L, f32 = DEPTH, np.float32
    o = {"x": np.ascontiguousarray(i["x"][0].T), "mem": np.ascontiguousarray(i["mem"][0].T),
         "positions": np.ascontiguousarray(i["positions"].reshape(1, SEQ))}
    half = ROPE // 2
    freq = np.float32(10000.0) ** (-np.arange(half, dtype=f32) / half)
    o["freq"] = np.stack([np.tile(freq.astype(f32), P // half),
                          np.tile(np.repeat(np.array([-1, 1], f32), half), P // ROPE)], axis=1)
    mask, t = np.zeros((32, 2, SEQ), f32), np.arange(SEQ)
    for b in range(NT):
        mask[b, 0] = t // CHUNK == 2 * b
        mask[b, 1, t // CHUNK == 2 * b + 1] = NEG
    o["mask"] = mask
    w = i["w_in"]
    kr = w[..., QR + KVR:QR + KVR + ROPE]
    rest = w[..., QR + KVR + ROPE:]
    w_in = np.concatenate([w[..., :QR + KVR], np.tile(kr, (1, 1, 4)), np.tile(swap_halves(kr), (1, 1, 4)),
                           rest], axis=-1)
    proj = [column_tiles(x) for x in (w_in, i["w_out"], i["w_mkv"], i["w_mq"], i["w_mo"], i["w_pq"])]
    o["proj"] = np.concatenate(proj, axis=1)
    u = i["peer_u"].reshape(L, EB, P, KT, P).transpose(0, 1, 4, 3, 2).reshape(L, EB, P, D)
    o["experts"] = np.concatenate([u, i["peer_v"].reshape(L, EB, P, D)], axis=1)

    def tiles(x):
        x = x.reshape(L, -1)
        return x.reshape(L, -1, P).transpose(0, 2, 1)
    log_step = np.broadcast_to(i["ssm_log_step"][:, :, None], (L, SG, SS))
    src = {"g_cq": i["g_cq"], "g_ckv": i["g_ckv"], "g_mix": i["g_mix"], "b_glu": i["b_glu"],
           "ssm_d": i["ssm_d"], "lam_re": i["ssm_lam_re"], "lam_im": i["ssm_lam_im"], "log_step": log_step,
           **{k: i[k] for k in ("ln_mix_g", "ln_mix_b", "ln_mem_g", "ln_mem_b", "ln_ffn_g", "ln_ffn_b")}}
    o["par"] = np.concatenate([tiles(src[k]) for k in PAR], axis=2)
    uq = i["w_uq"].reshape(L, QR, MH, NOPE + ROPE)
    nope, rope = uq[..., :NOPE].reshape(L, QR, -1), uq[..., NOPE:]
    uq = np.concatenate([nope, rope.reshape(L, QR, -1), swap_halves(rope).reshape(L, QR, -1)], axis=-1)
    o["uq"] = uq.reshape(L, 2, P, 768).transpose(0, 2, 1, 3).reshape(L, P, 2 * 768)
    ukv = i["w_ukv"].reshape(L, KVR, MH, NOPE + MV)
    o["ukv"] = np.concatenate([ukv[..., :NOPE].reshape(L, KVR, -1), ukv[..., NOPE:].reshape(L, KVR, -1)], axis=-1)
    o["glu"] = i["w_glu"].reshape(L, 3, P, 3 * P).transpose(0, 2, 1, 3).reshape(L, P, 9 * P)
    bz = np.zeros((L, P, 2, 3, 2, P), f32)
    cz = np.zeros((L, P, 2, ST, 2 * SC), f32)
    for z, (b, c) in enumerate(((i["ssm_b_re"], i["ssm_c_re"]), (i["ssm_b_im"], i["ssm_c_im"]))):
        for g in range(SG):
            st, gg = g // 2, g % 2
            r = 32 * (st % 4) + SC * gg
            bz[:, r:r + SC, z, st // 4, st % 2, SS * gg:SS * (gg + 1)] = b[:, g].transpose(0, 2, 1)
            cz[:, SS * gg:SS * (gg + 1), z, st, SC * gg:SC * (gg + 1)] = c[:, g].transpose(0, 2, 1)
    o["bz"], o["cz"] = bz.reshape(L, P, -1), cz.reshape(L, P, -1)
    o["keys"] = i["peer_sub_keys"].reshape(L, PH * 2, PK, P).transpose(0, 3, 1, 2)
    return {k: np.ascontiguousarray(v) for k, v in o.items()}


def kernel(**inputs):
    from concourse import bacc
    from concourse.bass_utils import run_bass_kernel_spmd

    arrays = layouts({k: np.asarray(v) for k, v in inputs.items()})
    nc = bacc.Bacc("TRN2", target_bir_lowering=False, num_devices=1)
    a = {k: nc.dram_tensor(k, v.shape, mybir.dt.from_np(v.dtype), kind="ExternalInput").ap()
         for k, v in arrays.items()}
    out = nc.dram_tensor("out", (D, SEQ), F32, kind="ExternalOutput").ap()
    program(nc, a, out)
    r = run_bass_kernel_spmd(nc, [arrays], core_ids=[0])
    return np.ascontiguousarray(r.results[0]["out"].T)[None]
```

```python
import math
from contextlib import ExitStack

import numpy as np
from concourse import bass, mybir

F32 = mybir.dt.float32
F16 = mybir.dt.float16
I32 = mybir.dt.int32
U32 = mybir.dt.uint32
ACT = mybir.ActivationFunctionType
ALU = mybir.AluOpType
AX = mybir.AxisListType

P = 128
D, SEQ, DEPTH = 1024, 512, 2
KT, NT = D // P, SEQ // P
QR, KVR = 256, 128
MH, NOPE, ROPE, MV = 6, 64, 32, 64
SG, SC, SS = 24, 16, 64
ST = SG * SS // P
BH, BD = 4, 64
MEM, XH, XD = 256, 4, 256
MT = MEM // P
PH, PK, TOP = 8, 128, 16
EB = PK
EPS = 1e-5
ALPHA = (2 * DEPTH) ** 0.25
MLA_SCALE = (NOPE + ROPE) ** -0.5
SB_SCALE = BD ** -0.5
MEM_SCALE = XD ** -0.5
CHUNK = 64
NEG = -1e30
LOWEST = -3e38

WS, XS = 256.0, 16.0
UNSCALE = 1.0 / (WS * XS)
GS = 4096.0

T_CQ, T_CKV, T_KR, T_KRS, T_U, T_QSB, T_KSB, T_VSB, T_OUT = 0, 2, 3, 4, 5, 8, 10, 12, 14
N_IN, N_OUT, N_MQ, N_MK, N_MV, N_MO, N_PQ = 14, 8, 8, 8, 8, 8, 16
T_MQ = N_IN + N_OUT
T_PQ = T_MQ + N_MQ + N_MK + N_MV + N_MO
N_PROJ = T_PQ + N_PQ
RING = 4


class Named:
    pass


class Steps:

    def __init__(self, eng, sem):
        self.eng, self.sem, self.n = eng, sem, 0

    def __call__(self, ins):
        self.n += 1
        ins.then_inc(self.sem, 1)
        self.eng.wait_ge(self.sem, self.n)

    def restart(self):
        self.eng.sem_clear(self.sem)
        self.n = 0



def load_tile(m, sp, src, r, k):
    sp.wait_ge(m.split_done, r * RING + k + 1)
    sp.dma_start(m.wf[:, k, :], src).then_inc(m.loaded[k], 16)


def split_high(m, act, r, k, slot=None):
    slot = k if slot is None else slot
    act.wait_ge(m.loaded[k], r * 16 + 16)
    act.wait_ge(m.tile_used, r * RING + k + 1)
    m.nc.scalar.activation(m.wh[:, slot, :], m.wf[:, k, :], ACT.Copy, scale=WS).then_inc(m.high_done, 1)


def split_low(m, dve, r, k, slot=None):
    slot = k if slot is None else slot
    dve.wait_ge(m.high_done, r * RING + k + 1)
    m.nc.vector.scalar_tensor_tensor(m.wl[:, slot, :], m.wf[:, k, :], WS, m.wh[:, slot, :],
                                     ALU.mult, ALU.subtract).then_inc(m.split_done, 1)



def prefetched_sp(m, sp):
    for k in range(RING):
        sp.sem_inc(m.loaded[k], 16)


def load_next(m, sp, tile, n):
    for k in range(RING):
        load_tile(m, sp, tile(k), (n + k) // RING, (n + k) % RING)


def split_next_high(m, act, n):
    act.wait_ge(m.tile_used, n + RING)
    for k in range(RING):
        act.wait_ge(m.loaded[(n + k) % RING], 16 * ((n + k) // RING) + 16)
        m.nc.scalar.activation(m.wh[:, k, :], m.wf[:, (n + k) % RING, :], ACT.Copy, scale=WS)\
            .then_inc(m.high_done, 1)


def split_next_low(m, dve, n):
    for k in range(RING):
        split_low(m, dve, (n + k) // RING, (n + k) % RING, k)


def wait_tile(m, pe, r, k):
    pe.wait_ge(m.split_done, r * RING + k + 1 + RING)


def project(m, out, slot, xh, xl, n):
    wh, wl = (w[:, slot, :].rearrange("p (k c) -> p k c", k=KT) for w in (m.wh, m.wl))
    for k in range(KT):
        m.nc.tensor.matmul(out, wh[:, k, :], xh[:, k, 0:n], start=(k == 0), stop=False)
        m.nc.tensor.matmul(out, wh[:, k, :], xl[:, k, 0:n], start=False, stop=False)
        last = m.nc.tensor.matmul(out, wl[:, k, :], xh[:, k, 0:n], start=False, stop=(k == KT - 1))
    return last


def project_rows(m, outs, slot, xh, xl):
    wh, wl = (w[:, slot, :].rearrange("p (k c) -> p k c", k=KT) for w in (m.wh, m.wl))
    for b, out in enumerate(outs):
        t = slice(b * P, (b + 1) * P)
        for k in range(KT):
            m.nc.tensor.matmul(out, xh[:, k, t], wh[:, k, :], start=(k == 0), stop=False)
            m.nc.tensor.matmul(out, xh[:, k, t], wl[:, k, :], start=False, stop=False)
            last = m.nc.tensor.matmul(out, xl[:, k, t], wh[:, k, :], start=False, stop=(k == KT - 1))
    return last



LN_CHUNKS = 4
LN_W = KT // LN_CHUNKS


def ln_pe(m, pe, bank_sum, bank_var):
    for f in range(KT):
        pe.wait_ge(m.res_added, f + 1)
        last = m.nc.tensor.matmul(bank_sum, m.ones[:, :], m.xT[:, f, :], start=(f == 0), stop=(f == KT - 1))
    last.then_inc(m.ln_sum, 1)
    for c in range(LN_CHUNKS):
        pe.wait_ge(m.ln_sq, c + 1)
        for f in range(LN_W):
            i = c * LN_W + f
            last = m.nc.tensor.matmul(bank_var, m.ones[:, :], m.sq[:, c % 2, f, :], start=(i == 0),
                                      stop=(i == KT - 1))
        last.then_inc(m.ln_var, 1)


def ln_act(m, act, bank_var, par, g, b):
    for c in range(LN_CHUNKS):
        act.wait_ge(m.ln_centred, c + 1)
        if c >= 2:
            act.wait_ge(m.ln_var, c - 1)
        m.nc.scalar.activation(m.sq[:, c % 2, :, :], m.xT[:, c * LN_W:(c + 1) * LN_W, :], ACT.Square)\
            .then_inc(m.ln_sq, 1)
    act.wait_ge(m.ln_var, LN_CHUNKS)
    m.nc.scalar.activation(m.rs[:, 0, :], bank_var, ACT.Sqrt, scale=1.0 / D, bias=m.eps_ln[:, :])\
        .then_inc(m.ln_sd, 1)
    act.wait_ge(m.ln_params, 1)
    for f in range(KT):
        act.wait_ge(m.ln_out, f // LN_W + 1)
        m.nc.scalar.activation(m.xh[:, f, :], m.xT[:, f, :], ACT.Identity, scale=m.gain[:, f:f + 1],
                               bias=m.bias[:, f:f + 1])
        m.nc.scalar.activation(m.xT[:, f, :], m.xT[:, f, :], ACT.Identity, scale=par[:, g][:, f:f + 1],
                               bias=par[:, b][:, f:f + 1]).then_inc(m.xh_done, 1)


def ln_params(m, dve, par, g, b):
    dve.wait_ge(m.params, 16)
    m.nc.vector.tensor_scalar(m.gain[:, :], par[:, g], XS, None, ALU.mult)
    m.nc.vector.tensor_scalar(m.bias[:, :], par[:, b], XS, None, ALU.mult).then_inc(m.ln_params, 1)


def ln_dve(m, dve, step, bank_sum):
    dve.wait_ge(m.ln_sum, 1)
    for c in range(LN_CHUNKS):
        x = m.xT[:, c * LN_W:(c + 1) * LN_W, :]
        mean = bank_sum.unsqueeze(1).to_broadcast([P, LN_W, SEQ])
        m.nc.vector.scalar_tensor_tensor(x, mean, -1.0 / D, x, ALU.mult, ALU.add).then_inc(m.ln_centred, 1)
    dve.wait_ge(m.ln_sd, 1)
    step(m.nc.vector.reciprocal(m.rs[:, 1, :], m.rs[:, 0, :]))
    dve.wait_ge(m.ln_centred, LN_CHUNKS)
    dve.wait_ge(m.ln_sq, LN_CHUNKS)
    for c in range(LN_CHUNKS):
        x = m.xT[:, c * LN_W:(c + 1) * LN_W, :]
        m.nc.vector.tensor_tensor(x, x, m.rs[:, 1:2, :].to_broadcast([P, LN_W, SEQ]), ALU.mult)\
            .then_inc(m.ln_out, 1)
    for f in range(KT):
        dve.wait_ge(m.xh_done, f + 1)
        step(m.nc.vector.scalar_tensor_tensor(m.xl[:, f, :], m.xT[:, f, :], XS, m.xh[:, f, :],
                                              ALU.mult, ALU.subtract))




TWO_PI = 2 * math.pi
PI_1 = 6.28125
PI_2 = float(np.float32(int((TWO_PI - PI_1) * 2 ** 21) / 2 ** 21))
PI_3 = TWO_PI - PI_1 - PI_2
ROUND = 1.5 * 2 ** 23
PI_IN = 3.1415925


def reduce_angle(nc, step, out, turns, ang, quarter):
    step(nc.vector.tensor_scalar(turns, ang, 1 / TWO_PI, 0.25 if quarter else 0.0, ALU.mult, ALU.add))
    step(nc.vector.tensor_scalar(turns, turns, ROUND, None, ALU.add))
    step(nc.vector.tensor_scalar(turns, turns, -ROUND, None, ALU.add))
    step(nc.vector.scalar_tensor_tensor(out, turns, -PI_1, ang, ALU.mult, ALU.add))
    step(nc.vector.scalar_tensor_tensor(out, turns, -PI_2, out, ALU.mult, ALU.add))
    step(nc.vector.scalar_tensor_tensor(out, turns, -PI_3, out, ALU.mult, ALU.add))
    if quarter:
        step(nc.vector.tensor_scalar(out, out, math.pi / 2, None, ALU.add))
    step(nc.vector.tensor_scalar(out, out, PI_IN, -PI_IN, ALU.min, ALU.max))


class Region:

    def __init__(self, tensor, words):
        self.tensor, self.words, self.at = tensor, words, 0

    def take(self, shape, dtype=F32):
        n = int(np.prod(shape)) // (2 if dtype == F16 else 1)
        assert self.at + n <= self.words, (self.at, n, self.words)
        v = self.tensor[:, self.at:self.at + n]
        self.at += n
        if dtype != F32:
            v = v.bitcast(dtype)
        if len(shape) > 1:
            names = "abcd"[:len(shape)]
            v = v.rearrange("p (%s) -> p %s" % (" ".join(names), " ".join(names)),
                            **dict(zip(names, shape)))
        return v


PAR = {}
N_PAR = 0
for _name, _cols in (("g_cq", 2), ("g_ckv", 1), ("g_mix", KT), ("ln_mix_g", KT), ("ln_mix_b", KT),
                     ("ln_mem_g", KT), ("ln_mem_b", KT), ("ln_ffn_g", KT), ("ln_ffn_b", KT),
                     ("b_glu", 3), ("ssm_d", 3), ("lam_re", ST), ("lam_im", ST), ("log_step", ST)):
    PAR[_name] = slice(N_PAR, N_PAR + _cols)
    N_PAR += _cols


def setup(nc, m, a):
    w = Region(m.work, m.words)
    pos = w.take([SEQ], I32)
    posf, ang, turns, arg = (w.take([SEQ]) for _ in range(4))
    with nc.Block() as block:
        @block.sync
        def _(sp):
            sp.dma_start(m.xT[:, :, :], a.x.rearrange("(k p) t -> p k t", p=P)).then_inc(m.s_x, 16)
            sp.dma_start(m.freq[:, :], a.freq).then_inc(m.s_small, 16)
            sp.dma_start(pos[:, :], a.positions.partition_broadcast(P)).then_inc(m.s_small, 16)

        @block.gpsimd
        def _(pool):
            nc.gpsimd.memset(m.ones[:, :], 1.0)
            nc.gpsimd.memset(m.full[:, :], -1.0 / SB_SCALE)
            nc.gpsimd.memset(m.eps[:, :], EPS)
            nc.gpsimd.memset(m.eps_ln[:, :], EPS / ALPHA ** 2).then_inc(m.s_pool, 1)
            nc.gpsimd.iota(m.iota16[:, :], pattern=[[1, TOP]], base=0, channel_multiplier=0,
                           allow_small_or_imprecise_dtypes=True)
            nc.gpsimd.iota(m.iota_rep[:, :, :], pattern=[[1, P], [0, TC]], base=0, channel_multiplier=0,
                           allow_small_or_imprecise_dtypes=True).then_inc(m.s_pool, 1)
            pool.wait_ge(m.s_pool, 2)
            for out, src, op, base, step_, cm, fill in (
                    (m.ident, m.ones, ALU.is_equal, 0, -1, 1, 0.0),
                    (m.tri, m.full, ALU.is_ge, 0, -1, 1, 0.0),
                    (m.before, m.ones, ALU.is_gt, 0, 1, -1, 0.0)):
                nc.gpsimd.affine_select(out=out[:, :], in_=src[:, :], pattern=[[step_, P]], compare_op=op,
                                        fill=fill, base=base, channel_multiplier=cm)

        @block.vector
        def _(dve):
            step = Steps(dve, m.dve_step)
            dve.wait_ge(m.s_small, 32)
            step(nc.vector.tensor_copy(posf[:, :], pos[:, :]))
            step(nc.vector.tensor_scalar(ang[:, :], posf[:, :], m.freq[:, 0:1], None, ALU.mult))
            reduce_angle(nc, step, arg[:, :], turns[:, :], ang[:, :], False)
            step(nc.vector.tensor_copy(m.rs[:, 0, :], arg[:, :]))
            reduce_angle(nc, step, arg[:, :], turns[:, :], ang[:, :], True)
            nc.vector.tensor_copy(m.rs[:, 1, :], arg[:, :]).then_inc(m.s_ang, 1)
            dve.wait_ge(m.s_sin, 1)
            nc.vector.tensor_scalar(m.sinT[:, :], m.sinT[:, :], m.freq[:, 1:2], None, ALU.mult)
            for f in range(KT):
                dve.wait_ge(m.xh_done, f + 1)
                nc.vector.scalar_tensor_tensor(m.xl[:, f, :], m.xT[:, f, :], XS, m.xh[:, f, :],
                                               ALU.mult, ALU.subtract)

        @block.scalar
        def _(act):
            act.wait_ge(m.s_x, 16)
            for f in range(KT):
                nc.scalar.activation(m.xh[:, f, :], m.xT[:, f, :], ACT.Copy, scale=XS).then_inc(m.xh_done, 1)
            act.wait_ge(m.s_ang, 1)
            nc.scalar.activation(m.sinT[:, :], m.rs[:, 0, :], ACT.Sin).then_inc(m.s_sin, 1)
            nc.scalar.activation(m.cosT[:, :], m.rs[:, 1, :], ACT.Sin)


def end_stage(nc, m):
    nc.sync.sem_clear(range(m.sem_first, m.sem_last + 1))
    nc.all_engine_barrier()


def ssm_parameters(m, dve, step, par, v, c, cc):
    nc = m.nc
    lr, li, ls = (par[:, PAR[n]] for n in ("lam_re", "lam_im", "log_step"))
    TT, OP = nc.vector.tensor_tensor, ALU
    dve.wait_ge(m.ssm_exp, 1)
    step(TT(v.th, li, v.step, OP.mult))
    step(TT(v.lrs, lr, v.step, OP.mult))
    reduce_angle(nc, step, v.a0, v.t0, v.th, False)
    reduce_angle(nc, step, v.a1, v.t0, v.th, True)
    dve.sem_inc(m.ssm_args, 1)
    dve.wait_ge(m.ssm_trig, 1)
    step(TT(v.re, v.r, v.cos, OP.mult))
    step(TT(v.im, v.r, v.sin, OP.mult))
    step(nc.vector.tensor_scalar(v.re, v.re, -1.0, None, OP.add))
    step(TT(v.t0, lr, lr, OP.mult))
    step(TT(v.t1, li, li, OP.mult))
    step(TT(v.t0, v.t0, v.t1, OP.add))
    step(nc.vector.reciprocal(v.inv, v.t0))
    step(TT(v.t0, v.re, lr, OP.mult))
    step(TT(v.t1, v.im, li, OP.mult))
    step(TT(v.t0, v.t0, v.t1, OP.add))
    step(TT(v.fre, v.t0, v.inv, OP.mult))
    step(TT(v.t0, v.im, lr, OP.mult))
    step(TT(v.t1, v.re, li, OP.mult))
    step(TT(v.t0, v.t0, v.t1, OP.subtract))
    step(TT(v.fim, v.t0, v.inv, OP.mult))
    dve.wait_ge(m.weights, 16 * N_SMALL)
    wide = [P, ST, 2 * SC]
    fre, fim = (x.unsqueeze(2).to_broadcast(wide) for x in (v.fre, v.fim))
    t = v.wide
    step(TT(t[:, 0], c[:, 0], fre, OP.mult))
    step(TT(t[:, 1], c[:, 1], fim, OP.mult))
    step(TT(cc[:, 0], t[:, 0], t[:, 1], OP.subtract))
    step(TT(cc[:, 1], t[:, 1], t[:, 0], OP.subtract))
    step(TT(t[:, 0], c[:, 0], fim, OP.mult))
    step(TT(t[:, 1], c[:, 1], fre, OP.mult))
    step(nc.vector.scalar_tensor_tensor(cc[:, 2], t[:, 0], -1.0, t[:, 1], OP.mult, OP.subtract))


N_SMALL = 6
PAIRS = ST // 2


def sb_cols(a):
    return {0: 0, 1: 512, 3: 896, 2: 1024}[a], SEQ - P * a


SB_W = 1280


def mixer(nc, m, a, layer):
    w = Region(m.work, m.words)
    par = w.take([N_PAR])
    lat = w.take([3, SEQ])
    cq, ckv = lat[:, 0:2, :], lat[:, 2:3, :]
    glu = lat.rearrange("p a t -> p (a t)")[:, 0:9 * P].rearrange("p (a c) -> p a c", a=3)
    kr, u = w.take([2, SEQ]), w.take([3, SEQ])
    qsb, ksb, vsb = w.take([2, SEQ]), w.take([2, SEQ]), w.take([NT, BH * BD])
    qh, kh, vm = w.take([MH, SEQ]), w.take([MH, SEQ]), w.take([NT, MH * MV])
    uq, ukv = w.take([2, 768]), w.take([768])
    bz = w.take([2, 3, 2, P])
    cc = w.take([3, ST, 2 * SC])
    tab = [x.rearrange("p k t -> p (k t)").bitcast(F32).rearrange("p (z a t) -> p z a t", z=2, a=2)
           for x in (m.xh[:, :, :], m.xl[:, :, :])]
    both = w.take([4, SEQ])
    vv, gg = both[:, 0:2, :], both[:, 2:4, :]
    grs = both[:, 0:3, :]
    sqs, sig = kh[:, 0:4, :], m.sqf[:, 0:3, :]
    share = w.at
    sp_, rl, wt = w.take([SB_W]), w.take([SB_W]), w.take([SB_W])
    w.at = share
    prob, probT = w.take([2, SEQ]), w.take([2, SEQ])
    w.at = share
    rt, cz = w.take([4, SEQ]), w.take([2, ST, 2 * SC])
    pr = m.sq
    small = Region(m.small, 2624)
    tmp = small.take([2, 2, SEQ // 2])
    v = Named()
    (v.step, v.th, v.lrs, v.a0, v.a1, v.t0, v.t1, v.sin, v.cos, v.r, v.re, v.im, v.inv, v.fre,
     v.fim) = (small.take([ST]) for _ in range(15))
    v.wide = small.take([2, ST, 2 * SC])
    mx, nmx, rsum, rinv = (small.take([2]) for _ in range(4))
    y = [qh[:, 2 * j, :] for j in range(3)] + [u[:, j, :] for j in range(3)] + [qsb[:, j, :] for j in range(2)]
    B = [m.ps[:, b, :] for b in range(8)]
    TT, STT, TS = nc.vector.tensor_tensor, nc.vector.scalar_tensor_tensor, nc.vector.tensor_scalar
    MM = nc.tensor.matmul
    EVAC = N_IN + 10
    dest = [cq[:, 0, :], cq[:, 1, :], ckv[:, 0, :], kr[:, 0, :], kr[:, 1, :], u[:, 0, :], u[:, 1, :],
            u[:, 2, :], qsb[:, 0, :], qsb[:, 1, :], ksb[:, 0, :], ksb[:, 1, :]]
    iters = [(h, b) for h in range(MH) for b in range(NT)]

    with nc.Block() as block:
        @block.sync
        def _(sp):
            sp.dma_start(par[:, :], a.par[layer]).then_inc(m.params, 16)
            for n in range(N_IN + N_OUT):
                load_tile(m, sp, a.proj[layer, n], n // RING, n % RING)
                if n == 3:
                    for dst, src in ((uq, a.uq), (ukv, a.ukv), (bz, a.bz), (cz, a.cz)):
                        flat = dst if len(dst.shape) == 2 else dst.rearrange(
                            {3: "p a b -> p (a b)", 4: "p a b c -> p (a b c)",
                             5: "p a b c d -> p (a b c d)"}[len(dst.shape)])
                        sp.dma_start(flat, src[layer]).then_inc(m.weights, 16)
                    for z, dst in enumerate((qh, kh)):
                        sp.dma_start(dst[96:P, :, :], a.mask[:, z:z + 1, :].to_broadcast([32, MH, SEQ]))\
                            .then_inc(m.weights, 16)
            load_next(m, sp, lambda k: a.proj[layer, T_MQ + k], N_IN + N_OUT)

        @block.tensor
        def _(pe):
            pe.sem_inc(m.tile_used, RING)
            for n in range(N_IN):
                wait_tile(m, pe, n // RING, n % RING)
                if n >= 2:
                    pe.wait_ge(m.evac, n - 1)
                if n < T_VSB:
                    last = project(m, B[n % 2], n % RING, m.xh, m.xl, SEQ)
                else:
                    last = project_rows(m, [B[n % 2][:, b * P:(b + 1) * P] for b in range(NT)], n % RING,
                                        m.xh, m.xl)
                last.then_inc(m.tile_used, 1)
                if n == T_KRS + 1:
                    pe.wait_ge(m.lat_sq, 2)
                    for c in range(2):
                        MM(B[2], m.ones[:, :], rt[:, c, :], start=(c == 0), stop=(c == 1))
                    pe.wait_ge(m.lat_sq, 3)
                    MM(B[3], m.ones[:, :], rt[:, 2, :], start=True, stop=True).then_inc(m.lat_sum, 1)
            pe.wait_ge(m.weights, 16 * N_SMALL)
            pe.wait_ge(m.lat_done, 3)
            for i in range(3):
                pe.wait_ge(m.evac, N_IN + i - 1)
                for c in range(2):
                    last = MM(B[(N_IN + i) % 2], uq[:, c, i * P:(i + 1) * P], cq[:, c, :],
                              start=(c == 0), stop=(c == 1))
                last.then_inc(m.up, 1)
            for i in range(3):
                pe.wait_ge(m.evac, N_IN + 3 + i - 1)
                MM(B[(N_IN + 3 + i) % 2], ukv[:, i * P:(i + 1) * P], ckv[:, 0, :], start=True, stop=True)\
                    .then_inc(m.up, 1)
            for b in range(NT):
                pe.wait_ge(m.evac, N_IN + 6 + b - 1)
                MM(B[(N_IN + 6 + b) % 2][:, 0:MH * MV], ckv[:, 0, b * P:(b + 1) * P], ukv[:, MH * NOPE:],
                   start=True, stop=True).then_inc(m.up, 1)
            for r in range(2):
                for s in range(2):
                    o = MH * NOPE + (2 * s + r) * 96
                    for c in range(2):
                        last = MM(B[4 + 2 * r + s][0:96, :], uq[:, c, o:o + 96], cq[:, c, :],
                                  start=(c == 0), stop=(c == 1))
                last.then_inc(m.rot, 1)
            pe.wait_ge(m.rot_done, 1)
            pe.wait_ge(m.evac, EVAC)

            def ssm_in(st):
                j, q = st // 4, st % 4
                if st >= 1:
                    pe.wait_ge(m.ssm_mul, st)
                rows = slice(64 * (q // 2), 64 * (q // 2) + 64)
                for z in range(2):
                    last = MM(B[z], bz[rows, z, j, q % 2, :], u[rows, j, :], start=True, stop=True)
                last.then_inc(m.ssm_bu, 1)

            def ssm_out(st):
                j, q = st // 4, st % 4
                pe.wait_ge(m.ssm_prod, st + 1)
                if q == 0 and j >= 1:
                    pe.wait_ge(m.ssm_y, j)
                out = B[2][32 * q:32 * q + 32, :]
                for i, (z, lhs) in enumerate((((0, 0), 0), ((1, 1), 1), ((1, 0), 2), ((0, 1), 2))):
                    last = MM(out, cc[:, lhs, st, :], pr[:, z[0], z[1], :], start=(i == 0), stop=(i == 3))
                last.then_inc(m.ssm_read, 1)

            def sb_scores(h, stop):
                rows = slice(64 * (h % 2), 64 * (h % 2) + 64)
                for s in range(NT):
                    o, n = sb_cols(s)
                    last = MM(m.zb[:, o:o + n], ksb[rows, h // 2, s * P:(s + 1) * P],
                              qsb[rows, h // 2, s * P:], start=True, stop=True)
                return last

            def sb_values(h):
                rows = slice(64 * (h % 2), 64 * (h % 2) + 64)
                pe.wait_ge(m.sb_wm, h + 1)
                if h == 2:
                    pe.wait_ge(m.sb_y, 1)
                for s in range(NT):
                    o, n = sb_cols(s)
                    last = MM(B[7][rows, s * P:], vsb[:, s, h * BD:(h + 1) * BD], wt[:, o:o + n],
                              start=(s == 0), stop=(s == NT - 1))
                last.then_inc(m.sb_o, 1)

            for h in range(BH):
                ssm_in(h)
                if h >= 1:
                    pe.wait_ge(m.sb_w, h)
                sb_scores(h, True).then_inc(m.sb_z, 1)
                if h >= 1:
                    sb_values(h - 1)
                    ssm_out(h - 1)
                pe.wait_ge(m.sb_sp, h + 1)
                rows = slice(64 * (h % 2), 64 * (h % 2) + 64)
                for s in range(NT):
                    o, n = sb_cols(s)
                    MM(m.zb[:, o:o + n], ksb[rows, h // 2, s * P:(s + 1) * P], qsb[rows, h // 2, s * P:],
                       start=True, stop=False)
                    last = MM(m.zb[:, o:o + n], m.tri[:, :], sp_[:, o:o + n], start=False, stop=(s == NT - 1))
                    for s2 in range(s + 1, NT):
                        o2, n2 = sb_cols(s2)
                        last = MM(m.zb[:, o + n - n2:o + n], m.full[:, :], sp_[:, o2:o2 + n2],
                                  start=False, stop=(s2 == NT - 1))
                last.then_inc(m.sb_t, 1)
            ssm_in(BH)
            ssm_out(BH - 1)
            sb_values(BH - 1)

            def mla_s(i):
                h, b = iters[i]
                if i >= 2:
                    pe.wait_ge(m.mla_e, i - 1)
                n = P * (b + 1)
                MM(B[4 + i % 2][:, 0:n], qh[:, h, b * P:n], kh[:, h, 0:n], start=True, stop=True)\
                    .then_inc(m.mla_sc, 1)

            def mla_t(i):
                h, b = iters[i]
                pe.wait_ge(m.mla_p, i + 1)
                if i >= 2:
                    pe.wait_ge(m.mla_pt, i - 1)
                for c in range(b + 1):
                    last = nc.tensor.transpose(B[(3, 6)[i % 2]][:, c * P:(c + 1) * P],
                                               prob[:, i % 2, c * P:(c + 1) * P], m.ident[:, :])
                last.then_inc(m.mla_tr, 1)

            def mla_o(i):
                h, b = iters[i]
                pe.wait_ge(m.mla_pt, i + 1)
                if h % 2 == 0 and b == 0:
                    if h == 0:
                        pe.wait_ge(m.sb_y, 2)
                    else:
                        pe.wait_ge(m.mla_y, h // 2)
                rows = slice(64 * (h % 2), 64 * (h % 2) + 64)
                for c in range(b + 1):
                    last = MM(B[7][rows, b * P:(b + 1) * P], vm[:, c, h * MV:(h + 1) * MV],
                              probT[:, i % 2, c * P:(c + 1) * P], start=(c == 0), stop=(c == b))
                last.then_inc(m.mla_av, 1)

            mla_s(0)
            for i in range(len(iters)):
                if i + 1 < len(iters):
                    mla_s(i + 1)
                if i % 3 == 0 and i >= 3:
                    ssm_out(BH + i // 3 - 1)
                if i >= 1:
                    mla_t(i - 1)
                if i >= 2:
                    mla_o(i - 2)
                if i % 3 == 1 and BH + i // 3 + 1 < ST:
                    ssm_in(BH + i // 3 + 1)
            mla_t(len(iters) - 1)
            mla_o(len(iters) - 2)
            mla_o(len(iters) - 1)
            ssm_out(ST - 1)

            def squares(i, g, c, n):
                pe.wait_ge(m.grp_sq, i + 1)
                MM(B[4 + g], m.ones[:, :], sqs[:, i % 4, :], start=(c == 0), stop=(c == n - 1))\
                    .then_inc(m.grp_sum, 1)

            for i, x in enumerate([(1, c, 2) for c in range(2)] + [(0, c, 3) for c in range(3)]):
                squares(i, *x)
            pe.wait_ge(m.glu_in, 16)
            pe.wait_ge(m.gelu_done, 3)
            for j in range(3):
                for c in range(3):
                    last = MM(B[j], glu[:, c, j * P:(j + 1) * P], u[:, c, :], start=(c == 0), stop=(c == 2))
                last.then_inc(m.glu_mm, 1)
            for c in range(3):
                squares(5 + c, 2, c, 3)
            for f in range(N_OUT):
                n = N_IN + f
                if f == 0:
                    pe.wait_ge(m.yl_done, KT)
                wait_tile(m, pe, n // RING, n % RING)
                if f >= 2:
                    pe.wait_ge(m.res_added, f - 1)
                project(m, B[f % 2], n % RING, m.xh, m.xl, SEQ).then_inc(m.tile_used, 1)
            ln_pe(m, pe, B[2], B[3])

        @block.scalar
        def _(act):
            AF = nc.scalar.activation
            act.wait_ge(m.params, 16)
            AF(v.step, par[:, PAR["log_step"]], ACT.Exp).then_inc(m.ssm_exp, 1)
            for n in range(RING):
                split_high(m, act, 0, n)
            for n in range(N_IN):
                act.wait_ge(m.tile_used, n + 1 + RING)
                if n < T_VSB:
                    AF(dest[n], B[n % 2], ACT.Copy, scale=UNSCALE).then_inc(m.evac, 1)
                else:
                    c = (n - T_VSB) * P
                    AF(vsb[:, :, c:c + P], B[n % 2].rearrange("p (b c) -> p b c", b=NT), ACT.Copy,
                       scale=UNSCALE).then_inc(m.evac, 1)
                if n < N_IN + N_OUT - RING:
                    split_high(m, act, (n + RING) // RING, n % RING)
                if n <= 2:
                    act.wait_ge(m.evac, n + 1)
                    AF(rt[:, n, :], dest[n], ACT.Square).then_inc(m.lat_sq, 1)
                if n == T_KRS + 2:
                    act.wait_ge(m.lat_sum, 1)
                    AF(m.rs[:, 0, :], B[2], ACT.Sqrt, scale=1.0 / QR, bias=m.eps[:, :])
                    AF(m.rs[:, 1, :], B[3], ACT.Sqrt, scale=1.0 / KVR, bias=m.eps[:, :]).then_inc(m.lat_sd, 1)
            act.wait_ge(m.ssm_args, 1)
            AF(v.sin, v.a0, ACT.Sin)
            AF(v.cos, v.a1, ACT.Sin)
            AF(v.r, v.lrs, ACT.Exp).then_inc(m.ssm_trig, 1)
            for i in range(10):
                act.wait_ge(m.up, i + 1)
                bank = B[(N_IN + i) % 2]
                if i < 6:
                    for z in range(2):
                        last = AF((qh, kh)[i // 3][0:NOPE, 2 * (i % 3) + z, :], bank[64 * z:64 * z + 64, :], ACT.Copy)
                else:
                    last = AF(vm[:, i - 6, :], bank[:, 0:MH * MV], ACT.Copy)
                last.then_inc(m.evac, 1)
            act.wait_ge(m.rot_done, 1)
            act.dma_start(glu, a.glu[layer].rearrange("p (a c) -> p a c", a=3)).then_inc(m.glu_in, 16)
            for h in range(BH):
                act.wait_ge(m.sb_z, h + 1)
                if h >= 1:
                    act.wait_ge(m.sb_t, h)
                AF(sp_[:, :], m.zb[:, 0:SB_W], ACT.Abs, scale=SB_SCALE).then_inc(m.act_step, 1)
                act.wait_ge(m.act_step, 3 * h + 1)
                AF(sp_[:, :], sp_[:, :], ACT.Exp, scale=-1.0).then_inc(m.act_step, 1)
                act.wait_ge(m.act_step, 3 * h + 2)
                AF(sp_[:, :], sp_[:, :], ACT.Ln, bias=1.0).then_inc(m.act_step, 1)
                if h == 2:
                    act.wait_ge(m.sb_o, h)
                    AF(y[6], B[7], ACT.Copy).then_inc(m.sb_y, 1)
                act.wait_ge(m.sb_t, h + 1)
                if h >= 1:
                    act.wait_ge(m.sb_o, h)
                AF(wt[:, :], m.zb[:, 0:SB_W], ACT.Exp, scale=SB_SCALE).then_inc(m.sb_w, 1)
            act.wait_ge(m.sb_o, BH)
            AF(y[7], B[7], ACT.Copy).then_inc(m.sb_y, 1)
            for i, (h, b) in enumerate(iters):
                n = P * (b + 1)
                act.wait_ge(m.mla_nm, i + 1)
                if i >= 2:
                    act.wait_ge(m.mla_tr, i - 1)
                if i == 0:
                    act.wait_ge(m.sb_o, BH)
                AF(prob[:, i % 2, 0:n], B[4 + i % 2][:, 0:n], ACT.Exp, scale=MLA_SCALE,
                   bias=nmx[:, i % 2:i % 2 + 1], accum_out=rsum[:, i % 2:i % 2 + 1]).then_inc(m.mla_e, 1)
                if i >= 1:
                    mla_copy(m, act, i - 1, iters, probT, B)
                if i >= 3 and iters[i - 3][1] == NT - 1 and iters[i - 3][0] % 2 == 1:
                    mla_out(m, act, i - 3, iters, y, B)
            mla_copy(m, act, len(iters) - 1, iters, probT, B)
            mla_out(m, act, len(iters) - 1, iters, y, B)
            order = [6, 7, 0, 1, 2, 3, 4, 5]

            def square(i):
                if i >= 4:
                    act.wait_ge(m.grp_sum, i - 3)
                AF(sqs[:, i % 4, :], y[order[i]], ACT.Square).then_inc(m.grp_sq, 1)

            def rms(k, need, width):
                act.wait_ge(m.grp_sum, need)
                if k == 1:
                    act.wait_ge(m.ssm_prod, ST)
                AF(grs[:, k, :], B[4 + k], ACT.Sqrt, scale=1.0 / width, bias=m.eps[:, :]).then_inc(m.grp_sd, 1)

            def high(i):
                act.wait_ge(m.y_norm, i + 1)
                AF(m.xh[:, order[i], :], y[order[i]], ACT.Copy, scale=XS).then_inc(m.yh_done, 1)

            act.wait_ge(m.sb_y, 2)
            act.wait_ge(m.mla_y, 3)
            for i in range(5):
                square(i)
            rms(1, 2, BH * BD)
            rms(0, 5, MH * MV)
            for j in range(3):
                act.wait_ge(m.ssm_y, j + 1)
                AF(u[:, j, :], u[:, j, :], ACT.Gelu_apprx_tanh).then_inc(m.gelu_done, 1)
            act.wait_ge(m.tile_used, N_IN + RING)
            for i in range(5):
                high(i)
            for j in range(3):
                act.wait_ge(m.glu_mm, j + 1)
                AF(sig[:, j, :], B[j], ACT.Sigmoid, bias=par[:, PAR["b_glu"]][:, j:j + 1]).then_inc(m.glu_sig, 1)
            for j in range(3):
                act.wait_ge(m.glu_done, j + 1)
                square(5 + j)
            rms(2, 8, SG * SC)
            for i in range(5, KT):
                high(i)
            for f in range(N_OUT - RING):
                n = N_IN + RING + f
                split_high(m, act, n // RING, n % RING)
            split_next_high(m, act, N_IN + N_OUT)
            ln_act(m, act, B[3], par, PAR["ln_mix_g"], PAR["ln_mix_b"])

        @block.gpsimd
        def _(pool):
            PT = nc.gpsimd.tensor_tensor
            step = Steps(pool, m.pool_step)
            pool.wait_ge(m.ssm_trig, 1)
            pool.wait_ge(m.tile_used, N_IN + RING)
            for q in range(PAIRS):
                c, s = tab[q % 2][:, 0], tab[q % 2][:, 1]
                if q >= 2:
                    pool.wait_ge(m.ssm_prod, 2 * (q - 1))
                nc.gpsimd.memset(c[:, :, 0:1], 1.0)
                nc.gpsimd.memset(s[:, :, 0:1], 0.0)
                nc.gpsimd.tensor_copy(c[:, :, 1:2], v.cos[:, 2 * q:2 * q + 2].unsqueeze(2))
                step(nc.gpsimd.tensor_copy(s[:, :, 1:2], v.sin[:, 2 * q:2 * q + 2].unsqueeze(2)))
                n = 1
                while n < SEQ:
                    k = min(n, SEQ - 1 - n)
                    lo, hi = slice(1, 1 + k), slice(n + 1, n + 1 + k)
                    cn, sn = (x[:, :, n:n + 1].to_broadcast([P, 2, k]) for x in (c, s))
                    t0, t1 = (tmp[:, z, :, 0:k] for z in range(2))
                    PT(t0, c[:, :, lo], cn, ALU.mult)
                    step(PT(t1, s[:, :, lo], sn, ALU.mult))
                    step(PT(c[:, :, hi], t0, t1, ALU.subtract))
                    PT(t0, s[:, :, lo], cn, ALU.mult)
                    step(PT(t1, c[:, :, lo], sn, ALU.mult))
                    step(PT(s[:, :, hi], t0, t1, ALU.add))
                    n *= 2
                pool.sem_inc(m.table, 1)

        @block.vector
        def _(dve):
            step = Steps(dve, m.dve_step)
            dve.sem_inc(m.split_done, RING)
            for n in range(RING):
                split_low(m, dve, 0, n)
            for n in range(N_IN):
                split_low(m, dve, (n + RING) // RING, n % RING)
            dve.wait_ge(m.lat_sd, 1)
            step(nc.vector.reciprocal(m.rs[:, :, :], m.rs[:, :, :]))
            for c in range(2):
                STT(cq[:, c, :], cq[:, c, :], par[:, PAR["g_cq"]][:, c:c + 1], m.rs[:, 0, :], ALU.mult,
                    ALU.mult).then_inc(m.lat_done, 1)
            STT(ckv[:, 0, :], ckv[:, 0, :], par[:, PAR["g_ckv"]], m.rs[:, 1, :], ALU.mult, ALU.mult)\
                .then_inc(m.lat_done, 1)
            ssm_parameters(m, dve, step, par, v, cz, cc)
            dve.wait_ge(m.evac, T_KRS + 1)
            TT(rt[:, 0, :], kr[:, 0, :], m.cosT[:, :], ALU.mult)
            step(TT(rt[:, 1, :], kr[:, 1, :], m.sinT[:, :], ALU.mult))
            step(TT(kh[64:96, :, :], rt[64:96, 0:1, :].to_broadcast([32, MH, SEQ]),
                    rt[64:96, 1:2, :].to_broadcast([32, MH, SEQ]), ALU.add))
            for r in range(2):
                dve.wait_ge(m.rot, r + 1)
                TT(rt[0:96, 2, :], B[4 + 2 * r][0:96, :], m.cosT[0:96, :], ALU.mult)
                step(TT(rt[0:96, 3, :], B[5 + 2 * r][0:96, :], m.sinT[0:96, :], ALU.mult))
                for z in range(3):
                    last = TT(qh[64:96, 3 * r + z, :], rt[32 * z:32 * z + 32, 2, :],
                              rt[32 * z:32 * z + 32, 3, :], ALU.add)
                step(last)
            dve.sem_inc(m.rot_done, 1)

            def ssm_forward(st):
                c, s = (tab[(st // 2) % 2][:, z, st % 2, :].unsqueeze(1).to_broadcast([P, 2, SEQ])
                        for z in range(2))
                dve.wait_ge(m.table, st // 2 + 1)
                dve.wait_ge(m.ssm_bu, st + 1)
                if st >= 1:
                    dve.wait_ge(m.ssm_read, st)
                TT(pr[:, 0], m.ps[:, 0:2, :], c, ALU.mult)
                TT(pr[:, 1], m.ps[:, 0:2, :], s, ALU.mult).then_inc(m.ssm_mul, 1)
                dve.wait_ge(m.ssm_mul, st + 1)
                TT(vv[:, 0, :], pr[:, 0, 0, :], pr[:, 1, 1, :], ALU.add)
                step(TT(vv[:, 1, :], pr[:, 0, 1, :], pr[:, 1, 0, :], ALU.subtract))

            def ssm_scan(st):
                decay = v.r[:, st:st + 1].to_broadcast([P, SEQ])
                for z in range(2):
                    last = nc.vector.tensor_tensor_scan(gg[:, z, :], decay, vv[:, z, :], 0.0, ALU.mult, ALU.add)
                step(last)

            def ssm_back(st):
                c, s = (tab[(st // 2) % 2][:, z, st % 2, :].unsqueeze(1).to_broadcast([P, 2, SEQ])
                        for z in range(2))
                TT(pr[:, 0], gg[:, :, :], c, ALU.mult)
                TT(pr[:, 1], gg[:, :, :], s, ALU.mult).then_inc(m.ssm_prod, 1)

            def ssm_skip(st):
                if st > 0 and st % 4 == 3:
                    j = st // 4
                    dve.wait_ge(m.ssm_read, st + 1)
                    STT(u[:, j, :], u[:, j, :], par[:, PAR["ssm_d"]][:, j:j + 1], B[2], ALU.mult, ALU.add)\
                        .then_inc(m.ssm_y, 1)

            for h in range(BH):
                ssm_forward(h)
                dve.wait_ge(m.act_step, 3 * h + 1)
                step(TS(rl[:, :], m.zb[:, 0:SB_W], SB_SCALE, 0.0, ALU.mult, ALU.max))
                ssm_scan(h)
                dve.wait_ge(m.act_step, 3 * (h + 1))
                step(TT(sp_[:, :], sp_[:, :], rl[:, :], ALU.add))
                for s in range(NT):
                    o, _n = sb_cols(s)
                    last = TT(sp_[:, o:o + P], sp_[:, o:o + P], m.before[:, :], ALU.mult)
                last.then_inc(m.sb_sp, 1)
                ssm_back(h)
                ssm_skip(h - 1)
                dve.wait_ge(m.sb_w, h + 1)
                for s in range(NT):
                    o, _n = sb_cols(s)
                    last = TT(wt[:, o:o + P], wt[:, o:o + P], m.before[:, :], ALU.mult)
                last.then_inc(m.sb_wm, 1)
            ssm_skip(BH - 1)
            for i, (h, b) in enumerate(iters):
                n, k = P * (b + 1), i % 2
                dve.wait_ge(m.mla_sc, i + 1)
                step(nc.vector.reduce_max(mx[:, k:k + 1], B[4 + k][:, 0:n], AX.X))
                if i >= 2:
                    dve.wait_ge(m.mla_e, i - 1)
                TS(nmx[:, k:k + 1], mx[:, k:k + 1], -MLA_SCALE, None, ALU.mult).then_inc(m.mla_nm, 1)
                st = BH + i // 3
                if i % 3 == 0:
                    if i >= 3:
                        ssm_skip(st - 1)
                    ssm_forward(st)
                elif i % 3 == 1:
                    ssm_scan(st)
                else:
                    ssm_back(st)
                dve.wait_ge(m.mla_e, i + 1)
                step(nc.vector.reciprocal(rinv[:, k:k + 1], rsum[:, k:k + 1]))
                TS(prob[:, k, 0:n], prob[:, k, 0:n], rinv[:, k:k + 1], None, ALU.mult).then_inc(m.mla_p, 1)
            ssm_skip(ST - 1)
            order = [6, 7, 0, 1, 2, 3, 4, 5]

            def norm(k, need, tiles):
                dve.wait_ge(m.grp_sd, need)
                step(nc.vector.reciprocal(grs[:, k, :], grs[:, k, :]))
                for i in tiles:
                    f = order[i]
                    STT(y[f], y[f], par[:, PAR["g_mix"]][:, f:f + 1], grs[:, k, :], ALU.mult, ALU.mult)\
                        .then_inc(m.y_norm, 1)

            def low(i):
                f = order[i]
                dve.wait_ge(m.yh_done, i + 1)
                STT(m.xl[:, f, :], y[f], XS, m.xh[:, f, :], ALU.mult, ALU.subtract).then_inc(m.yl_done, 1)

            norm(1, 1, (0, 1))
            norm(0, 2, (2, 3, 4))
            for i in range(5):
                low(i)
            for j in range(3):
                dve.wait_ge(m.glu_sig, j + 1)
                dve.wait_ge(m.glu_mm, 3)
                TT(u[:, j, :], u[:, j, :], sig[:, j, :], ALU.mult).then_inc(m.glu_done, 1)
            dve.wait_ge(m.grp_sq, 8)
            norm(2, 3, (5, 6, 7))
            for i in range(5, KT):
                low(i)
            for f in range(N_OUT):
                if f < N_OUT - RING:
                    n = N_IN + RING + f
                    split_low(m, dve, n // RING, n % RING)
                dve.wait_ge(m.tile_used, N_IN + f + 1 + RING)
                STT(m.xT[:, f, :], B[f % 2], UNSCALE / ALPHA, m.xT[:, f, :], ALU.mult, ALU.add)\
                    .then_inc(m.res_added, 1)
            ln_params(m, dve, par, PAR["ln_mix_g"], PAR["ln_mix_b"])
            split_next_low(m, dve, N_IN + N_OUT)
            ln_dve(m, dve, step, B[2])
    end_stage(nc, m)


def mla_copy(m, act, i, iters, probT, B):
    n = P * (iters[i][1] + 1)
    act.wait_ge(m.mla_tr, i + 1)
    if i >= 2:
        act.wait_ge(m.mla_av, i - 1)
    m.nc.scalar.activation(probT[:, i % 2, 0:n], B[(3, 6)[i % 2]][:, 0:n], ACT.Copy).then_inc(m.mla_pt, 1)


def mla_out(m, act, i, iters, y, B):
    act.wait_ge(m.mla_av, i + 1)
    m.nc.scalar.activation(y[iters[i][0] // 2], B[7], ACT.Copy).then_inc(m.mla_y, 1)


def memory(nc, m, a, layer):
    w = Region(m.work, m.words)
    par = w.take([N_PAR])
    memf = w.take([KT, MEM])
    mh, ml = w.take([KT, MEM], F16), w.take([KT, MEM], F16)
    km, vm, q = w.take([KT, MEM]), w.take([MT, D]), w.take([KT, SEQ])
    prob, probT = w.take([2, MEM]), w.take([2, MT, SEQ])
    small = Region(m.small, 1400)
    mx, nmx, rsum, rinv = (small.take([2]) for _ in range(4))
    B = [m.ps[:, b, :] for b in range(8)]
    STT, TS = nc.vector.scalar_tensor_tensor, nc.vector.tensor_scalar
    MM = nc.tensor.matmul
    iters = [(h, b) for h in range(XH) for b in range(NT)]
    R_MK, R_MV, R_MO = N_MQ // RING, (N_MQ + N_MK) // RING, (N_MQ + N_MK + N_MV) // RING
    R_END = R_MO + N_MO // RING
    PAIR = XD // P

    with nc.Block() as block:
        @block.sync
        def _(sp):
            prefetched_sp(m, sp)
            sp.dma_start(memf[:, :, :], a.mem.rearrange("(k p) t -> p k t", p=P)).then_inc(m.weights, 16)
            sp.dma_start(par[:, :], a.par[layer]).then_inc(m.params, 16)
            with sp.Fori(1, R_END) as r:
                for k in range(RING):
                    load_tile(m, sp, a.proj[layer, r * RING + (T_MQ + k)], r, k)
            load_next(m, sp, lambda k: a.proj[layer, T_PQ + k], R_END * RING)

        @block.tensor
        def _(pe):
            pe.sem_inc(m.tile_used, RING)

            def segment(r0, emit):
                with pe.Fori(r0, r0 + 2) as r:
                    for k in range(RING):
                        wait_tile(m, pe, r, k)
                        pe.wait_ge(m.evac, r * RING + k + 1)
                        emit(k).then_inc(m.tile_used, 1)

            segment(0, lambda k: project(m, B[k % 2], k, m.xh, m.xl, SEQ))
            pe.wait_ge(m.weights, 17)
            segment(R_MK, lambda k: project(m, B[k % 2][:, 0:MEM], k, mh, ml, MEM))
            segment(R_MV, lambda k: project_rows(m, [B[k % 2][:, b * P:(b + 1) * P] for b in range(MT)],
                                                 k, mh, ml))
            pe.wait_ge(m.evac, R_MO * RING + 2)

            def scores(i):
                h, b = iters[i]
                if i >= 2:
                    pe.wait_ge(m.mla_e, i - 1)
                for c in range(PAIR):
                    last = MM(B[2 + i % 2][:, 0:MEM], q[:, PAIR * h + c, b * P:(b + 1) * P],
                              km[:, PAIR * h + c, :], start=(c == 0), stop=(c == PAIR - 1))
                last.then_inc(m.mla_sc, 1)

            def turn(i):
                pe.wait_ge(m.mla_p, i + 1)
                if i >= 2:
                    pe.wait_ge(m.mla_pt, i - 1)
                for c in range(MT):
                    last = nc.tensor.transpose(B[4 + i % 2][:, c * P:(c + 1) * P],
                                               prob[:, i % 2, c * P:(c + 1) * P], m.ident[:, :])
                last.then_inc(m.mla_tr, 1)

            def values(h):
                pe.wait_ge(m.mla_pt, NT * (h + 1))
                for f in range(PAIR):
                    n = PAIR * h + f
                    if n >= 2:
                        pe.wait_ge(m.yl_done, n - 1)
                    for c in range(MT):
                        last = MM(B[6 + f], vm[:, c, n * P:(n + 1) * P], probT[:, h % 2, c, :],
                                  start=(c == 0), stop=(c == MT - 1))
                    last.then_inc(m.mla_av, 1)

            for i, (h, b) in enumerate(iters):
                scores(i)
                if i >= 1:
                    turn(i - 1)
                if b == 1 and h >= 1:
                    values(h - 1)
            turn(len(iters) - 1)
            values(XH - 1)
            for f in range(N_MO):
                if f == 0:
                    pe.wait_ge(m.yl_done, KT)
                wait_tile(m, pe, R_MO + f // RING, f % RING)
                if f >= 2:
                    pe.wait_ge(m.res_added, f - 1)
                project(m, B[f % 2], f % RING, m.xh, m.xl, SEQ).then_inc(m.tile_used, 1)
            ln_pe(m, pe, B[2], B[3])

        @block.scalar
        def _(act):
            AF = nc.scalar.activation
            act.sem_inc(m.evac, 2)
            act.sem_inc(m.high_done, RING)
            act.wait_ge(m.weights, 16)
            AF(mh[:, :, :], memf[:, :, :], ACT.Copy, scale=XS).then_inc(m.xh_mem, 1)

            def segment(r0, dst):
                with act.Fori(0, 2) as s:
                    for k in range(RING):
                        act.wait_ge(m.tile_used, s * RING + (r0 * RING + k + 1 + RING))
                        dst(s, k).then_inc(m.evac, 1)
                        split_high(m, act, s + (r0 + 1), k)

            segment(0, lambda s, k: AF(q[:, bass.ds(s * RING + k, 1), :],
                                       m.ps[:, k % 2:k % 2 + 1, :], ACT.Copy, scale=UNSCALE))
            segment(R_MK, lambda s, k: AF(km[:, bass.ds(s * RING + k, 1), :],
                                       m.ps[:, k % 2:k % 2 + 1, 0:MEM], ACT.Copy, scale=UNSCALE))
            segment(R_MV, lambda s, k: AF(vm[:, :, bass.ds((s * RING + k) * P, P)],
                                          B[k % 2][:, 0:MEM].rearrange("p (b c) -> p b c", b=MT),
                                          ACT.Copy, scale=UNSCALE))

            def exps(i):
                act.wait_ge(m.mla_nm, i + 1)
                if i >= 2:
                    act.wait_ge(m.mla_tr, i - 1)
                AF(prob[:, i % 2, :], B[2 + i % 2][:, 0:MEM], ACT.Exp, scale=MEM_SCALE,
                   bias=nmx[:, i % 2:i % 2 + 1], accum_out=rsum[:, i % 2:i % 2 + 1]).then_inc(m.mla_e, 1)

            def copy(i):
                h, b = iters[i]
                act.wait_ge(m.mla_tr, i + 1)
                if h >= 2 and b == 0:
                    act.wait_ge(m.mla_av, PAIR * (h - 1))
                AF(probT[:, h % 2, :, b * P:(b + 1) * P],
                   B[4 + i % 2][:, 0:MEM].rearrange("p (c t) -> p c t", c=MT), ACT.Copy)\
                    .then_inc(m.mla_pt, 1)

            def high(h):
                for f in range(PAIR):
                    n = PAIR * h + f
                    act.wait_ge(m.mla_av, n + 1)
                    AF(m.xh[:, n, :], B[6 + f], ACT.Copy, scale=XS).then_inc(m.yh_done, 1)

            for i, (h, b) in enumerate(iters):
                exps(i)
                if i >= 1:
                    copy(i - 1)
                if b == 2 and h >= 1:
                    high(h - 1)
            copy(len(iters) - 1)
            high(XH - 1)
            for k in range(RING):
                split_high(m, act, R_END - 1, k)
            split_next_high(m, act, R_END * RING)
            ln_act(m, act, B[3], par, PAR["ln_mem_g"], PAR["ln_mem_b"])

        @block.vector
        def _(dve):
            step = Steps(dve, m.dve_step)
            dve.sem_inc(m.split_done, 2 * RING)
            dve.wait_ge(m.xh_mem, 1)
            STT(ml[:, :, :], memf[:, :, :], XS, mh[:, :, :], ALU.mult, ALU.subtract).then_inc(m.weights, 1)
            with dve.Fori(1, R_MO + 1) as r:
                for k in range(RING):
                    split_low(m, dve, r, k)

            def low(h):
                for f in range(PAIR):
                    n = PAIR * h + f
                    dve.wait_ge(m.yh_done, n + 1)
                    STT(m.xl[:, n, :], B[6 + f], XS, m.xh[:, n, :], ALU.mult, ALU.subtract)\
                        .then_inc(m.yl_done, 1)

            for i, (h, b) in enumerate(iters):
                k = i % 2
                dve.wait_ge(m.mla_sc, i + 1)
                step(nc.vector.reduce_max(mx[:, k:k + 1], B[2 + k][:, 0:MEM], AX.X))
                if i >= 2:
                    dve.wait_ge(m.mla_e, i - 1)
                TS(nmx[:, k:k + 1], mx[:, k:k + 1], -MEM_SCALE, None, ALU.mult).then_inc(m.mla_nm, 1)
                dve.wait_ge(m.mla_e, i + 1)
                step(nc.vector.reciprocal(rinv[:, k:k + 1], rsum[:, k:k + 1]))
                TS(prob[:, k, :], prob[:, k, :], rinv[:, k:k + 1], None, ALU.mult).then_inc(m.mla_p, 1)
                if b == 3 and h >= 1:
                    low(h - 1)
            low(XH - 1)
            for f in range(N_MO):
                if f < RING:
                    split_low(m, dve, R_END - 1, f)
                dve.wait_ge(m.tile_used, R_MO * RING + f + 1 + RING)
                STT(m.xT[:, f, :], B[f % 2], UNSCALE / ALPHA, m.xT[:, f, :], ALU.mult, ALU.add)\
                    .then_inc(m.res_added, 1)
            ln_params(m, dve, par, PAR["ln_mem_g"], PAR["ln_mem_b"])
            split_next_low(m, dve, R_END * RING)
            ln_dve(m, dve, step, B[2])
    end_stage(nc, m)


TC = 8
CPT = P // TC
R_PQ = N_PQ // RING
R_SEL = 3
R_CHUNK = 2
R_TOK = R_SEL + 2 + R_CHUNK
R_LAST = EB // RING - NT * R_TOK
STORES = 8
TURN = RING - 1


def share(j):
    return range(j * 2 * PH // (R_SEL * RING), (j + 1) * 2 * PH // (R_SEL * RING))

CPH = CPT // (R_CHUNK * RING)


def select(nc, m, a, layer):
    w = Region(m.work, m.words)
    scores = w.take([NT, PH * 2, PK])
    stage = w.take([PK, P])
    keys = stage.rearrange("p a b -> p (a b)")[:, 0:PH * 2 * PK].rearrange("p (h n) -> p h n", h=PH * 2)
    qb, gst = w.take([2, SEQ]), w.take([2, SEQ])
    hot = m.sq.rearrange("p a b t -> p (a b t)").bitcast(F16)
    hot2 = qb.rearrange("p a t -> p (a t)").bitcast(F16)
    hot3 = w.take([2 * P * TC], F16)
    eqb = [hot[:, z * P * TC:(z + 1) * P * TC].rearrange("p (i t) -> p i t", i=P) for z in range(2)]
    ahi = [hot[:, (2 + z) * P * TC:(3 + z) * P * TC].rearrange("p (i t) -> p i t", i=P) for z in range(2)]
    alo = [hot2[:, z * P * TC:(z + 1) * P * TC].rearrange("p (i t) -> p i t", i=P) for z in range(2)]
    bhot = [hot3[:, z * P * TC:(z + 1) * P * TC].rearrange("p (i t) -> p i t", i=P) for z in range(2)]
    eqf = m.sq.rearrange("p a b t -> p (a b t)").rearrange("p (h s c) -> p h s c", h=PH, s=TOP)
    s = Region(m.small, 1400 + 1024)
    sin = s.take([2, PK])
    wk, wk2 = s.take([PK]), s.take([TOP * TOP])
    cand = s.take([TOP, TOP])
    tv, ti, tif = s.take([PH * 2, TOP]), s.take([PH * 2, TOP], U32), s.take([PH * 2, TOP])
    bv, bp = s.take([PH, TOP]), s.take([PH, TOP], U32)
    gsum, ginv = s.take([PH]), s.take([PH])
    gate, first, second = (m.rs[:, :, :].rearrange("p a t -> p (a t)")[:, z * P:(z + 1) * P] for z in range(3))
    ib = m.rs[:, :, :].rearrange("p a t -> p (a t)")[:, 3 * P:4 * P].bitcast(U32)
    ibf = m.rs[:, :, :].rearrange("p a t -> p (a t)")[:, 4 * P:5 * P]
    tr = m.rs[:, :, :].rearrange("p a t -> p (a t)")[:, 5 * P:7 * P].bitcast(F16)
    firstT, secondT, ghi, glo = (tr[:, z * P:(z + 1) * P] for z in range(4))
    B = [m.ps[:, b, :] for b in range(8)]
    TT, STT, TS = nc.vector.tensor_tensor, nc.vector.scalar_tensor_tensor, nc.vector.tensor_scalar
    MM = nc.tensor.matmul

    with nc.Block() as block:
        @block.sync
        def _(sp):
            sp.dma_start(keys, a.keys[layer]).then_inc(m.weights, 16)
            prefetched_sp(m, sp)
            with sp.Fori(1, R_PQ) as r:
                for k in range(RING):
                    load_tile(m, sp, a.proj[layer, r * RING + (T_PQ + k)], r, k)
            with sp.Fori(0, EB // RING + 1) as r:
                for k in range(RING):
                    load_tile(m, sp, a.experts[layer, r * RING + k], r + R_PQ, k)

        @block.tensor
        def _(pe):
            pe.sem_inc(m.tile_used, RING)
            pe.sem_inc(m.scored, 2)
            pe.sem_inc(m.spread, 2)
            pe.wait_ge(m.weights, 16)

            def score(r, k):
                pe.wait_ge(m.evac, r * RING + (k + 1 + 2))
                pe.wait_ge(m.sc_copied, r * RING + (k + 1))
                for b in range(NT):
                    last = MM(B[2 + k % 2][:, b * P:(b + 1) * P], qb[:, k % 2, b * P:(b + 1) * P],
                              keys[:, bass.ds(r * RING + k, 1), :].rearrange("p a n -> p (a n)"),
                              start=True, stop=True)
                last.then_inc(m.scored, 1)

            def projected(r, k):
                wait_tile(m, pe, r, k)
                pe.wait_ge(m.evac, r * RING + (k + 1))
                project(m, B[k % 2], k, m.xh, m.xl, SEQ).then_inc(m.tile_used, 1)

            with pe.Fori(0, R_PQ) as r:
                for k in range(RING):
                    projected(r, k)
                    if k:
                        score(r, k - 1)
                score(r, RING - 1)
            with pe.Fori(0, NT) as tt:
                with pe.Fori(0, R_SEL + 1) as i:
                    for k in range(RING):
                        projected(tt * R_TOK + i + R_PQ, k)
                for k in range(TURN):
                    projected(tt * R_TOK + (R_PQ + R_SEL + 1), k)
                pe.wait_ge(m.selected, tt + 1)
                for z, x in enumerate((first, second, gate)):
                    last = nc.tensor.transpose(B[2][:, z * P:(z + 1) * P], x, m.ident[:, :])
                last.then_inc(m.sel_turned, 1)
                for k in range(TURN, RING):
                    projected(tt * R_TOK + (R_PQ + R_SEL + 1), k)
                with pe.Fori(0, R_CHUNK) as i:
                    for k in range(RING):
                        projected(tt * R_TOK + i + (R_PQ + R_SEL + 2), k)
                        for c in range(k * CPH, (k + 1) * CPH):
                            n = tt * CPT + i * (RING * CPH) + (c + 1)
                            pe.wait_ge(m.hot, n)
                            pe.wait_ge(m.staged, n)
                            for t in range(TC):
                                out = B[4 + 2 * (c % 2) + t // 4][:, (t % 4) * P:(t % 4 + 1) * P]
                                MM(out, bhot[c % 2][:, :, t], ahi[c % 2][:, :, t], start=True, stop=False)
                                last = MM(out, bhot[c % 2][:, :, t], alo[c % 2][:, :, t], start=False,
                                          stop=True)
                            last.then_inc(m.spread, 1)
            with pe.Fori(0, R_LAST) as i:
                for k in range(RING):
                    projected(i + (R_PQ + NT * R_TOK), k)

        @block.scalar
        def _(act):
            AF = nc.scalar.activation
            act.sem_inc(m.evac, 2)
            act.sem_inc(m.staged, 2)
            act.sem_inc(m.stage_free, 1)
            for s in m.g_out:
                act.sem_inc(s, 1)
            act.sem_inc(m.high_done, RING)
            with act.Fori(0, R_PQ) as r:
                for k in range(RING):
                    act.wait_ge(m.tile_used, r * RING + (k + 1 + RING))
                    act.wait_ge(m.scored, r * RING + (k + 1))
                    AF(qb[:, k % 2, :], B[k % 2], ACT.Copy, scale=UNSCALE).then_inc(m.evac, 1)
                    split_high(m, act, r + 1, k)

            def hidden(r, k):
                act.wait_ge(m.tile_used, r * RING + (k + 1 + RING))
                act.wait_ge(m.g_out[k % 2], (r - R_PQ) * 32 + (16 * (k // 2) + 1))
                AF(gst[:, k % 2, :], B[k % 2], ACT.Gelu_apprx_tanh, scale=UNSCALE).then_inc(m.evac, 1)
                split_high(m, act, r + 1, k)
                act.wait_ge(m.evac, r * RING + (k + 1 + 2))
                act.dma_start(m.hid[r * RING + (k - R_PQ * RING)], gst[:, k % 2, :])\
                    .then_inc(m.g_out[k % 2], 16)

            act.wait_ge(m.sc_copied, N_PQ + 2)
            with act.Fori(0, NT) as tt:
                for j in range(R_SEL * RING):
                    hidden(tt * R_TOK + (j // RING + R_PQ), j % RING)
                    for hc in share(j):
                        act.wait_ge(m.sel_used, tt * 2 * PH + (hc + 1))
                        AF(sin[:, hc % 2:hc % 2 + 1, :],
                           scores[:, bass.ds(tt, 1), hc:hc + 1, :].rearrange("p a h n -> p (a h) n"),
                           ACT.Copy).then_inc(m.sel_in, 1)
                act.wait_ge(m.best, tt + 1)
                AF(gate, gate, ACT.Exp).then_inc(m.gate_e, 1)
                for k in range(RING):
                    hidden(tt * R_TOK + (R_PQ + R_SEL), k)
                for k in range(TURN):
                    hidden(tt * R_TOK + (R_PQ + R_SEL + 1), k)
                act.wait_ge(m.sel_turned, tt + 1)
                AF(firstT, B[2][:, 0:P], ACT.Copy).then_inc(m.sel_high, 1)
                AF(secondT, B[2][:, P:2 * P], ACT.Copy).then_inc(m.sel_high, 1)
                AF(ghi, B[2][:, 2 * P:3 * P], ACT.Copy, scale=GS).then_inc(m.sel_high, 1)
                act.wait_ge(m.stage_free, tt + 1)
                for k in range(TURN, RING):
                    hidden(tt * R_TOK + (R_PQ + R_SEL + 1), k)
                with act.Fori(0, R_CHUNK) as i:
                    for k in range(RING):
                        hidden(tt * R_TOK + i + (R_PQ + R_SEL + 2), k)
                        for c in range(k * CPH, (k + 1) * CPH):
                            n = i * (RING * CPH) + c
                            act.wait_ge(m.spread, tt * CPT + n + (1 + 2))
                            dst = stage.rearrange("p i t -> p t i")[:, bass.ds(n * TC, TC), :]
                            AF(dst, m.ps[:, 4 + 2 * (c % 2):6 + 2 * (c % 2), :].rearrange(
                                "p z (t i) -> p (z t) i", i=P), ACT.Copy, scale=1 / GS).then_inc(m.staged, 1)
            with act.Fori(0, R_LAST) as i:
                for k in range(RING):
                    hidden(i + (R_PQ + NT * R_TOK), k)
            for z in range(2):
                act.wait_ge(m.g_out[z], 16 * EB // 2 + 1)

        @block.gpsimd
        def _(pool):
            with pool.Fori(0, NT) as tt:
                pool.wait_ge(m.staged, tt * CPT + (CPT + 2))
                for c in range(STORES):
                    i = slice(c * EB // STORES, (c + 1) * EB // STORES)
                    pool.dma_start(m.gates[i, :, bass.ds(tt * P, P)].rearrange("i j t -> j i t"), stage[:, i, :])\
                        .then_inc(m.gates_out, 16)
                    pool.wait_ge(m.gates_out, layer * (16 * STORES * NT) + tt * (16 * STORES) + 16 * (c + 1))
                pool.sem_inc(m.stage_free, 1)

        @block.vector
        def _(dve):
            V = nc.vector
            step = Steps(dve, m.dve_step)
            dve.sem_inc(m.split_done, 2 * RING)
            dve.sem_inc(m.sc_copied, 2)
            dve.sem_inc(m.sel_used, 2)
            with dve.Fori(0, R_PQ) as r:
                for k in range(RING):
                    split_low(m, dve, r + 1, k)
                    dve.wait_ge(m.scored, r * RING + (k + 1 + 2))
                    V.tensor_copy(scores[:, :, bass.ds(r * RING + k, 1), :].rearrange("p b a n -> p b (a n)"),
                                  B[2 + k % 2].rearrange("p (b n) -> p b n", b=NT)).then_inc(m.sc_copied, 1)

            def top16(vals, idx, src, work):
                step(V.max(vals[:, 0:8], src))
                V.max_index(idx[:, 0:8], vals[:, 0:8], src)
                step(V.match_replace(work, vals[:, 0:8], src, LOWEST))
                step(V.max(vals[:, 8:16], work))
                return V.max_index(idx[:, 8:16], vals[:, 8:16], work)

            wide = [P, PH, TOP, TOP]

            def picked(out, side):
                step(V.tensor_copy(ibf, ib))
                place = ibf.rearrange("p (h s) -> p h s", h=PH).unsqueeze(3).to_broadcast(wide)
                step(TT(eqf, place, m.iota16[:, :].unsqueeze(1).unsqueeze(1).to_broadcast(wide), ALU.is_equal))
                step(TT(eqf, eqf, tif[:, side:PH * 2:2, :].unsqueeze(2).to_broadcast(wide), ALU.mult))
                return V.reduce_sum(out.rearrange("p (h s) -> p h s", h=PH), eqf, AX.X)

            with dve.Fori(0, NT) as tt:
                for j in range(R_SEL * RING):
                    step.restart()
                    dve.wait_ge(m.sel_in, tt * 2 * PH + share(j).stop)
                    split_low(m, dve, tt * R_TOK + (j // RING + R_PQ + 1), j % RING)
                    for hc in share(j):
                        top16(tv[:, hc, :], ti[:, hc, :], sin[:, hc % 2, :], wk).then_inc(m.sel_used, 1)
                        if hc % 2:
                            h = hc // 2
                            step(TT(cand[:, :, :], tv[:, hc - 1, :].unsqueeze(2).to_broadcast([P, TOP, TOP]),
                                    tv[:, hc, :].unsqueeze(1).to_broadcast([P, TOP, TOP]), ALU.add))
                            step(top16(bv[:, h, :], bp[:, h, :], cand.rearrange("p a b -> p (a b)"), wk2))
                r_pick = tt * R_TOK + (R_PQ + R_SEL + 1)
                gate3 = gate.rearrange("p (h s) -> p h s", h=PH)
                TT(gate3, bv[:, :, :], bv[:, :, 0:1].to_broadcast([P, PH, TOP]), ALU.subtract)\
                    .then_inc(m.best, 1)
                dve.wait_ge(m.best, tt + 1)
                V.tensor_copy(tif[:, :, :], ti[:, :, :])
                bpf = bp.rearrange("p h s -> p (h s)")
                step(TS(ib, bpf, 4, None, ALU.logical_shift_right))
                dve.wait_ge(m.spread, tt * CPT + 2)
                split_low(m, dve, r_pick, 0)
                step(picked(first, 0))
                split_low(m, dve, r_pick, 1)
                step(TS(ib, bpf, TOP - 1, None, ALU.bitwise_and))
                dve.wait_ge(m.gate_e, tt + 1)
                split_low(m, dve, r_pick, 2)
                step(V.reduce_sum(gsum, gate3, AX.X))
                step(V.reciprocal(ginv, gsum))
                TT(gate3, gate3, ginv.unsqueeze(2).to_broadcast([P, PH, TOP]), ALU.mult)
                picked(second, 1).then_inc(m.selected, 1)
                split_low(m, dve, r_pick, 3)
                for k in range(TURN):
                    split_low(m, dve, tt * R_TOK + (R_PQ + R_SEL + 2), k)
                dve.wait_ge(m.sel_high, tt * 3 + 3)
                step(STT(glo, B[2][:, 2 * P:3 * P], GS, ghi, ALU.mult, ALU.subtract))
                for k in range(TURN, RING):
                    split_low(m, dve, tt * R_TOK + (R_PQ + R_SEL + 2), k)
                with dve.Fori(0, R_CHUNK) as i:
                    step.restart()
                    for k in range(RING):
                        for c in range(k * CPH, (k + 1) * CPH):
                            n = i * (RING * CPH) + c
                            dve.wait_ge(m.spread, tt * CPT + n + 1)
                            t1, t2, hi, lo = (x[:, bass.ds(n * TC, TC)].unsqueeze(1)
                                              .to_broadcast([P, P, TC]) for x in (firstT, secondT, ghi, glo))
                            TT(eqb[c % 2], m.iota_rep[:, :, :], t1, ALU.is_equal)
                            step(TT(bhot[c % 2], m.iota_rep[:, :, :], t2, ALU.is_equal))
                            TT(ahi[c % 2], eqb[c % 2], hi, ALU.mult)
                            TT(alo[c % 2], eqb[c % 2], lo, ALU.mult).then_inc(m.hot, 1)
                        split_low(m, dve, tt * R_TOK + i + (R_PQ + R_SEL + 3), k)
            with dve.Fori(0, R_LAST) as i:
                for k in range(RING):
                    split_low(m, dve, i + (R_PQ + NT * R_TOK + 1), k)
    end_stage(nc, m)


GROUP = 4
NG = EB // GROUP


def outputs(nc, m, a, layer):
    w = Region(m.work, m.words)
    par = w.take([N_PAR])
    wh1, wl1 = w.take([RING, D], F16), w.take([RING, D], F16)
    gw = w.take([GROUP, 2, SEQ])
    ph, pl = w.take([2, GROUP, SEQ], F16), w.take([2, GROUP, SEQ], F16)
    wh, wl = (m.wh, wh1), (m.wl, wl1)
    B = [m.ps[:, b, :] for b in range(8)]
    TT, STT = nc.vector.tensor_tensor, nc.vector.scalar_tensor_tensor

    with nc.Block() as block:
        @block.sync
        def _(sp):
            sp.dma_start(par[:, :], a.par[layer]).then_inc(m.params, 16)

            def group(g, first=False):
                for b in range(GROUP):
                    if not first:
                        load_tile(m, sp, a.experts[layer, g * GROUP + (EB + b)], g, b)
                    sp.wait_ge(m.gw_used, g * GROUP + (b + 1))
                    sp.dma_start(gw[:, b, 0, :], m.hid[g * GROUP + b]).then_inc(m.gw_in[b], 16)
                    sp.dma_start(gw[:, b, 1, :], m.gates[g * GROUP + b]).then_inc(m.gw_in[b], 16)

            group(0, True)
            with sp.Fori(1, NG) as g:
                group(g)

        @block.tensor
        def _(pe):
            pe.sem_inc(m.out_done, KT)

            def first_group():
                for b in range(GROUP):
                    pe.wait_ge(m.split_done, b + 1 + RING)
                    pe.wait_ge(m.prod_done, b + 1)
                    for f in range(KT):
                        c = slice(f * P, (f + 1) * P)
                        if b == 0:
                            pe.wait_ge(m.out_added, f + 1)
                        nc.tensor.matmul(B[f], wh[0][:, b, c], ph[:, 0, b, :], start=(b == 0), stop=False)
                        nc.tensor.matmul(B[f], wh[0][:, b, c], pl[:, 0, b, :], start=False, stop=False)
                        last = nc.tensor.matmul(B[f], wl[0][:, b, c], ph[:, 0, b, :], start=False,
                                                stop=(b == GROUP - 1))
                        if b == GROUP - 1:
                            last.then_inc(m.out_done, 1)

            def group(g, z):
                pe.wait_ge(m.split_done, g * GROUP + (GROUP + RING))
                pe.wait_ge(m.prod_done, g * GROUP + GROUP)
                for f in range(KT):
                    pe.wait_ge(m.out_added, g * KT + (f + 1))
                    for b in range(GROUP):
                        c = slice(f * P, (f + 1) * P)
                        nc.tensor.matmul(B[f], wh[z][:, b, c], ph[:, z, b, :], start=(b == 0), stop=False)
                        nc.tensor.matmul(B[f], wh[z][:, b, c], pl[:, z, b, :], start=False, stop=False)
                        last = nc.tensor.matmul(B[f], wl[z][:, b, c], ph[:, z, b, :], start=False,
                                                stop=(b == GROUP - 1))
                    last.then_inc(m.out_done, 1)

            first_group()
            group(1, 1)
            with pe.Fori(1, NG // 2) as i:
                group(i * 2, 0)
                group(i * 2 + 1, 1)
            ln_pe(m, pe, B[0], B[1])

        @block.scalar
        def _(act):
            def group(g, z, first=False):
                for b in range(GROUP):
                    if not first:
                        act.wait_ge(m.loaded[b], g * 16)
                        act.wait_ge(m.out_done, g * KT)
                        nc.scalar.activation(wh[z][:, b, :], m.wf[:, b, :], ACT.Copy, scale=WS)\
                            .then_inc(m.high_done, 1)
                    act.wait_ge(m.multiplied, g * GROUP + (b + 1))
                    nc.scalar.activation(ph[:, z, b, :], gw[:, b, 0, :], ACT.Copy, scale=XS)\
                        .then_inc(m.prod_high, 1)

            group(0, 0, True)
            with act.Fori(0, NG // 2 - 1) as i:
                group(i * 2 + 1, 1)
                group(i * 2 + 2, 0)
            group(NG - 1, 1)
            ln_act(m, act, B[1], par, PAR["ln_ffn_g"], PAR["ln_ffn_b"])

        @block.vector
        def _(dve):
            step = Steps(dve, m.dve_step)
            dve.sem_inc(m.split_done, 2 * RING)
            dve.sem_inc(m.out_added, KT)
            dve.sem_inc(m.gw_used, GROUP)

            def add(g, f):
                dve.wait_ge(m.out_done, g * KT + (f + 1 + KT))
                return STT(m.xT[:, f, :], B[f], UNSCALE / ALPHA, m.xT[:, f, :], ALU.mult, ALU.add)

            def prepare(g, z, before, first=False):
                for b in range(GROUP):
                    dve.wait_ge(m.gw_in[b], g * 32 + 32)
                    TT(gw[:, b, 0, :], gw[:, b, 0, :], gw[:, b, 1, :], ALU.mult).then_inc(m.multiplied, 1)
                    if not first:
                        dve.wait_ge(m.high_done, g * GROUP + (b + 1 - GROUP))
                        STT(wl[z][:, b, :], m.wf[:, b, :], WS, wh[z][:, b, :], ALU.mult, ALU.subtract)\
                            .then_inc(m.split_done, 1)
                    dve.wait_ge(m.prod_high, g * GROUP + (b + 1))
                    STT(pl[:, z, b, :], gw[:, b, 0, :], XS, ph[:, z, b, :], ALU.mult, ALU.subtract)\
                        .then_inc(m.prod_done, 1)
                    dve.wait_ge(m.prod_done, g * GROUP + (b + 1))
                    dve.sem_inc(m.gw_used, 1)
                    if not first:
                        for f in (2 * b, 2 * b + 1):
                            add(before, f).then_inc(m.out_added, 1)

            prepare(0, 0, None, True)
            with dve.Fori(0, NG // 2 - 1) as i:
                prepare(i * 2 + 1, 1, i * 2)
                prepare(i * 2 + 2, 0, i * 2 + 1)
            prepare(NG - 1, 1, NG - 2)
            for f in range(KT):
                add(NG - 1, f).then_inc(m.res_added, 1)
            ln_params(m, dve, par, PAR["ln_ffn_g"], PAR["ln_ffn_b"])
            ln_dve(m, dve, step, B[0])
    end_stage(nc, m)


INPUTS = "x mem positions freq mask par proj experts keys uq ukv glu bz cz".split()
SEMAPHORES = """split_done tile_used high_done params weights s_x s_small s_pool s_ang s_sin evac lat_sq lat_sum
lat_done up rot rot_done ssm_exp ssm_args ssm_trig table ssm_bu ssm_mul ssm_prod ssm_read
ssm_y sb_z sb_sp sb_t sb_w sb_wm sb_o sb_y mla_sc mla_nm mla_e mla_p mla_tr mla_pt mla_av mla_y
gelu_done glu_in glu_mm glu_sig glu_done grp_sq grp_sum y_norm yh_done yl_done res_added
ln_sum ln_centred ln_sq ln_var ln_out ln_params ln_sd lat_sd grp_sd xh_done xh_mem act_step dve_step pool_step scored
sc_copied sel_in sel_used best gate_e selected sel_turned sel_high hot spread
staged stage_free gw_used multiplied prod_high prod_done out_added out_done""".split()


def program(nc, inputs, out, depth=DEPTH, stages=4):
    with ExitStack() as ctx:
        def sb(name, shape, dt=F32):
            return ctx.enter_context(nc.sbuf_tensor(name, shape, dt))

        a = Named()
        (a.x, a.mem, a.positions, a.freq, a.mask, a.par, a.proj, a.experts, a.keys, a.uq, a.ukv, a.glu, a.bz,
         a.cz) = (inputs[n] for n in INPUTS)
        m = Named()
        m.nc = nc
        sems = [ctx.enter_context(nc.semaphore(name)) for name in SEMAPHORES]
        (m.split_done, m.tile_used, m.high_done, m.params, m.weights, m.s_x, m.s_small, m.s_pool,
         m.s_ang, m.s_sin, m.evac, m.lat_sq, m.lat_sum, m.lat_done, m.up, m.rot, m.rot_done,
         m.ssm_exp, m.ssm_args, m.ssm_trig, m.table, m.ssm_bu, m.ssm_mul, m.ssm_prod, m.ssm_read,
         m.ssm_y, m.sb_z, m.sb_sp, m.sb_t, m.sb_w, m.sb_wm, m.sb_o, m.sb_y, m.mla_sc, m.mla_nm, m.mla_e,
         m.mla_p, m.mla_tr, m.mla_pt, m.mla_av, m.mla_y, m.gelu_done, m.glu_in, m.glu_mm, m.glu_sig,
         m.glu_done, m.grp_sq, m.grp_sum, m.y_norm, m.yh_done, m.yl_done, m.res_added,
         m.ln_sum, m.ln_centred, m.ln_sq, m.ln_var, m.ln_out, m.ln_params, m.ln_sd, m.lat_sd, m.grp_sd, m.xh_done, m.xh_mem, m.act_step,
         m.dve_step, m.pool_step, m.scored, m.sc_copied, m.sel_in, m.sel_used, m.best, m.gate_e,
         m.selected, m.sel_turned, m.sel_high, m.hot, m.spread, m.staged, m.stage_free,
         m.gw_used, m.multiplied, m.prod_high, m.prod_done, m.out_added, m.out_done) = sems
        m.loaded = [ctx.enter_context(nc.semaphore(f"loaded{k}")) for k in range(RING)]
        m.g_out = [ctx.enter_context(nc.semaphore(f"g_out{k}")) for k in range(2)]
        m.gw_in = [ctx.enter_context(nc.semaphore(f"gw_in{k}")) for k in range(GROUP)]
        nums = [s.num for s in [*sems, *m.loaded, *m.g_out, *m.gw_in]]
        m.sem_first, m.sem_last = min(nums), max(nums)
        assert m.sem_last - m.sem_first + 1 == len(nums)
        m.gates_out = ctx.enter_context(nc.semaphore("gates_out"))
        m.s_out = ctx.enter_context(nc.semaphore("s_out"))
        m.xT = sb("xT", [P, KT, SEQ])
        m.xh, m.xl = sb("xh", [P, KT, SEQ], F16), sb("xl", [P, KT, SEQ], F16)
        m.wf = sb("wf", [P, RING, D])
        m.wh, m.wl = sb("wh", [P, RING, D], F16), sb("wl", [P, RING, D], F16)
        m.sq = sb("sq", [P, 2, LN_W, SEQ])[:, :, :, :]
        m.sqf = m.sq.rearrange("p a b t -> p (a b) t")
        m.gain, m.bias = sb("gain", [P, KT]), sb("bias", [P, KT])
        m.rs = sb("rs", [P, 2, SEQ])
        m.ident, m.ones, m.full, m.tri, m.before = (
            sb(n, [P, P]) for n in ("ident", "ones", "full", "tri", "before"))
        m.eps, m.eps_ln, m.freq = sb("eps", [P, 1]), sb("eps_ln", [P, 1]), sb("freq_sb", [P, 2])
        m.iota16, m.iota_rep = sb("iota16", [P, TOP]), sb("iota_rep", [P, P, TC], F16)
        m.cosT, m.sinT = sb("cosT", [P, SEQ]), sb("sinT", [P, SEQ])
        m.small = sb("small", [P, 2624])
        m.words = 28100
        m.work = sb("work", [P, m.words])
        m.ps = ctx.enter_context(nc.psum_tensor("ps", [P, 8, SEQ], F32))
        m.zb = m.ps[:, 4:7, :].rearrange("p b t -> p (b t)")
        m.gates = nc.dram_tensor("gates", (EB, P, SEQ), F32, kind="Internal").ap()
        m.hid = nc.dram_tensor("hid", (EB, P, SEQ), F32, kind="Internal").ap()

        setup(nc, m, a)
        end_stage(nc, m)
        with nc.Fori(0, depth) as layer:
            for stage in (mixer, memory, select, outputs)[:stages]:
                stage(nc, m, a, layer)
        with nc.Block() as block:
            @block.sync
            def _(sp):
                sp.dma_start(out.rearrange("(k p) t -> p k t", p=P), m.xT[:, :, :]).then_inc(m.s_out, 16)
                sp.wait_ge(m.s_out, 16)



def column_tiles(w):
    n = w.shape[-1] // P
    return w.reshape(DEPTH, KT, P, n, P).transpose(0, 3, 2, 1, 4).reshape(DEPTH, n, P, KT * P)


def swap_halves(w):
    return np.concatenate([w[..., ROPE // 2:], w[..., :ROPE // 2]], axis=-1)


def layouts(i):
    L, f32 = DEPTH, np.float32
    o = {"x": np.ascontiguousarray(i["x"][0].T), "mem": np.ascontiguousarray(i["mem"][0].T),
         "positions": np.ascontiguousarray(i["positions"].reshape(1, SEQ))}
    half = ROPE // 2
    freq = np.float32(10000.0) ** (-np.arange(half, dtype=f32) / half)
    o["freq"] = np.stack([np.tile(freq.astype(f32), P // half),
                          np.tile(np.repeat(np.array([-1, 1], f32), half), P // ROPE)], axis=1)
    mask, t = np.zeros((32, 2, SEQ), f32), np.arange(SEQ)
    for b in range(NT):
        mask[b, 0] = t // CHUNK == 2 * b
        mask[b, 1, t // CHUNK == 2 * b + 1] = NEG
    o["mask"] = mask
    w = i["w_in"]
    kr = w[..., QR + KVR:QR + KVR + ROPE]
    rest = w[..., QR + KVR + ROPE:]
    w_in = np.concatenate([w[..., :QR + KVR], np.tile(kr, (1, 1, 4)), np.tile(swap_halves(kr), (1, 1, 4)),
                           rest], axis=-1)
    proj = [column_tiles(x) for x in (w_in, i["w_out"], i["w_mq"], i["w_mkv"], i["w_mo"], i["w_pq"])]
    o["proj"] = np.concatenate(proj, axis=1)
    u = i["peer_u"].reshape(L, EB, P, KT, P).transpose(0, 1, 4, 3, 2).reshape(L, EB, P, D)
    o["experts"] = np.concatenate([u, i["peer_v"].reshape(L, EB, P, D)], axis=1)

    def tiles(x):
        x = x.reshape(L, -1)
        return x.reshape(L, -1, P).transpose(0, 2, 1)
    log_step = np.broadcast_to(i["ssm_log_step"][:, :, None], (L, SG, SS))
    src = {"g_cq": i["g_cq"], "g_ckv": i["g_ckv"], "g_mix": i["g_mix"], "b_glu": i["b_glu"],
           "ssm_d": i["ssm_d"], "lam_re": i["ssm_lam_re"], "lam_im": i["ssm_lam_im"], "log_step": log_step,
           **{k: i[k] for k in ("ln_mix_g", "ln_mix_b", "ln_mem_g", "ln_mem_b", "ln_ffn_g", "ln_ffn_b")}}
    o["par"] = np.concatenate([tiles(src[k]) for k in PAR], axis=2)
    uq = i["w_uq"].reshape(L, QR, MH, NOPE + ROPE)
    nope, rope = uq[..., :NOPE].reshape(L, QR, -1), uq[..., NOPE:]
    uq = np.concatenate([nope, rope.reshape(L, QR, -1), swap_halves(rope).reshape(L, QR, -1)], axis=-1)
    o["uq"] = uq.reshape(L, 2, P, 768).transpose(0, 2, 1, 3).reshape(L, P, 2 * 768)
    ukv = i["w_ukv"].reshape(L, KVR, MH, NOPE + MV)
    o["ukv"] = np.concatenate([ukv[..., :NOPE].reshape(L, KVR, -1), ukv[..., NOPE:].reshape(L, KVR, -1)], axis=-1)
    o["glu"] = i["w_glu"].reshape(L, 3, P, 3 * P).transpose(0, 2, 1, 3).reshape(L, P, 9 * P)
    bz = np.zeros((L, P, 2, 3, 2, P), f32)
    cz = np.zeros((L, P, 2, ST, 2 * SC), f32)
    for z, (b, c) in enumerate(((i["ssm_b_re"], i["ssm_c_re"]), (i["ssm_b_im"], i["ssm_c_im"]))):
        for g in range(SG):
            st, gg = g // 2, g % 2
            r = 32 * (st % 4) + SC * gg
            bz[:, r:r + SC, z, st // 4, st % 2, SS * gg:SS * (gg + 1)] = b[:, g].transpose(0, 2, 1)
            cz[:, SS * gg:SS * (gg + 1), z, st, SC * gg:SC * (gg + 1)] = c[:, g].transpose(0, 2, 1)
    o["bz"], o["cz"] = bz.reshape(L, P, -1), cz.reshape(L, P, -1)
    o["keys"] = i["peer_sub_keys"].reshape(L, PH * 2, PK, P).transpose(0, 3, 1, 2)
    return {k: np.ascontiguousarray(v) for k, v in o.items()}


def kernel(**inputs):
    from concourse import bacc
    from concourse.bass_utils import run_bass_kernel_spmd

    arrays = layouts({k: np.asarray(v) for k, v in inputs.items()})
    nc = bacc.Bacc("TRN2", target_bir_lowering=False, num_devices=1)
    a = {k: nc.dram_tensor(k, v.shape, mybir.dt.from_np(v.dtype), kind="ExternalInput").ap()
         for k, v in arrays.items()}
    out = nc.dram_tensor("out", (D, SEQ), F32, kind="ExternalOutput").ap()
    program(nc, a, out)
    r = run_bass_kernel_spmd(nc, [arrays], core_ids=[0])
    return np.ascontiguousarray(r.results[0]["out"].T)[None]
```
